# Optimizing a Trainium2 kernel written in Bass

```python
import jax, jax.numpy as jnp
from jax import lax
import numpy as np

D_MODEL = 1024
BATCH = 1
SEQ = 1024
DEPTH = 1

N_MEM = 256
MLA_HEADS = 8
MLA_NOPE = 64
MLA_ROPE = 32
MLA_V = 64
MLA_Q_RANK = 256
MLA_KV_RANK = 128
MLA_WIDTH = MLA_HEADS * MLA_V
RET_HEADS = 4
RET_DK = 128
RET_DV = 128
RET_CHUNK = 128
RET_WIDTH = RET_HEADS * RET_DV
X_HEADS = 4
X_HEAD_DIM = D_MODEL // X_HEADS
D_FF = 2816
CONV_W = 3
Q_BLOCK = 128
ROPE_THETA = 10000.0
EPS = 1e-6
IN_WIDTH = MLA_Q_RANK + MLA_KV_RANK + MLA_ROPE + 2 * RET_HEADS * RET_DK + 2 * RET_WIDTH + 2 * D_MODEL

kernel_name = "hybrid_mla_retention_gated_block"

def rms_norm(x, g):
    xf = x.astype(jnp.float32)
    y = xf * lax.rsqrt(jnp.mean(xf * xf, axis=-1, keepdims=True) + EPS)
    return (y * g.astype(jnp.float32)).astype(x.dtype)

def rotary(x, positions):
    d = x.shape[-1]
    half = d // 2
    inv = ROPE_THETA ** (-jnp.arange(half, dtype=jnp.float32) / half)
    ang = positions.astype(jnp.float32)[:, :, None] * inv
    cos = jnp.cos(ang)[:, :, None, :]
    sin = jnp.sin(ang)[:, :, None, :]
    x1 = x[..., :half].astype(jnp.float32)
    x2 = x[..., half:].astype(jnp.float32)
    return jnp.concatenate([x1 * cos - x2 * sin, x2 * cos + x1 * sin], axis=-1).astype(x.dtype)

def causal_block_attention(q, k, v, scale):
    B, H, S, dq = q.shape
    dv = v.shape[-1]
    nb = S // Q_BLOCK
    qb = q.reshape(B, H, nb, Q_BLOCK, dq).transpose(2, 0, 1, 3, 4)
    kpos = jnp.arange(S)
    neg = jnp.finfo(jnp.float32).min

    def one(args):
        q_blk, i = args
        s = jnp.einsum('bhqd,bhkd->bhqk', q_blk, k).astype(jnp.float32) * scale
        qpos = i * Q_BLOCK + jnp.arange(Q_BLOCK)
        s = jnp.where(kpos[None, :] <= qpos[:, None], s, neg)
        p = jax.nn.softmax(s, axis=-1).astype(v.dtype)
        return jnp.einsum('bhqk,bhkd->bhqd', p, v)

    o = lax.map(one, (qb, jnp.arange(nb)))
    return o.transpose(1, 2, 0, 3, 4).reshape(B, H, S, dv)

def retention_chunkwise(q, k, v):
    B, S, H, dk = q.shape
    dv = v.shape[-1]
    C = RET_CHUNK
    nc = S // C
    log_g = jnp.log1p(-jnp.exp2(-5.0 - jnp.arange(H, dtype=jnp.float32)))
    idx = jnp.arange(C, dtype=jnp.float32)
    rel = idx[:, None] - idx[None, :]
    dmask = jnp.where(rel >= 0, jnp.exp(log_g[:, None, None] * jnp.maximum(rel, 0.0)), 0.0)
    zeta = jnp.exp(log_g[None, :] * (C - 1.0 - idx)[:, None])
    xi = jnp.exp(log_g[None, :] * (idx + 1.0)[:, None])
    chunk_decay = jnp.exp(log_g * C)

    qc = q.reshape(B, nc, C, H, dk)
    kc = k.reshape(B, nc, C, H, dk)
    vc = v.reshape(B, nc, C, H, dv)
    s = jnp.einsum('bcnhd,bcmhd->bchnm', qc, kc) * dmask.astype(q.dtype)[None, None]
    inner = jnp.einsum('bchnm,bcmhe->bcnhe', s, vc)
    kv = jnp.einsum('bcmhd,bcmhe->cbhde', kc * zeta.astype(q.dtype)[None, None, :, :, None], vc).astype(jnp.float32)

    def step(R, kv_c):
        return R * chunk_decay[None, :, None, None] + kv_c, R

    _, R_prev = lax.scan(step, jnp.zeros((B, H, dk, dv), jnp.float32), kv)
    cross = jnp.einsum('bcnhd,cbhde->bcnhe', qc * xi.astype(q.dtype)[None, None, :, :, None], R_prev.astype(q.dtype))
    return (inner + cross).reshape(B, S, H, dv)

def head_group_norm(y, g):
    B, S, H, d = y.shape
    yf = y.astype(jnp.float32)
    mu = jnp.mean(yf, axis=-1, keepdims=True)
    var = jnp.mean(jnp.square(yf - mu), axis=-1, keepdims=True)
    yn = ((yf - mu) * lax.rsqrt(var + EPS)).reshape(B, S, H * d)
    return (yn * g.astype(jnp.float32)).astype(y.dtype)

def causal_dwconv(u, w, b):
    C = u.shape[-1]
    y = lax.conv_general_dilated(u, w[:, None, :].astype(u.dtype), window_strides=(1,),
                                 padding=[(CONV_W - 1, 0)],
                                 dimension_numbers=('NWC', 'WIO', 'NWC'),
                                 feature_group_count=C)
    return y + b

def setup_inputs(seed: int = 0) -> dict:
    key = jax.random.key(seed)
    ks = jax.random.split(key, 32)
    f32 = jnp.float32
    L = DEPTH

    def w(k, shape, fan_in):
        return jax.random.normal(k, shape, f32) * (fan_in ** -0.5)

    def gain(k, shape):
        return 1.0 + 0.05 * jax.random.normal(k, shape, f32)

    x = jax.random.normal(ks[0], (BATCH, SEQ, D_MODEL), f32)
    mem = jax.random.normal(ks[1], (BATCH, N_MEM, D_MODEL), f32)
    positions = jnp.broadcast_to(jnp.arange(SEQ, dtype=jnp.int32)[None, :], (BATCH, SEQ))
    return {
        "x": x,
        "mem": mem,
        "positions": positions,
        "g_mix": gain(ks[2], (L, D_MODEL)),
        "w_in": w(ks[3], (L, D_MODEL, IN_WIDTH), D_MODEL),
        "b_gate": 0.01 * jax.random.normal(ks[4], (L, 2 * D_MODEL), f32),
        "g_q_lat": gain(ks[5], (L, MLA_Q_RANK)),
        "w_uq": w(ks[6], (L, MLA_Q_RANK, MLA_HEADS * (MLA_NOPE + MLA_ROPE)), MLA_Q_RANK),
        "g_kv_lat": gain(ks[7], (L, MLA_KV_RANK)),
        "w_ukv": w(ks[8], (L, MLA_KV_RANK, MLA_HEADS * (MLA_NOPE + MLA_V)), MLA_KV_RANK),
        "w_proj_mla": w(ks[9], (L, MLA_WIDTH, D_MODEL), MLA_WIDTH),
        "g_ret": gain(ks[10], (L, RET_WIDTH)),
        "w_proj_ret": w(ks[11], (L, RET_WIDTH, D_MODEL), RET_WIDTH),
        "w_out": w(ks[12], (L, D_MODEL, D_MODEL), D_MODEL),
        "g_cross": gain(ks[13], (L, D_MODEL)),
        "g_mem": gain(ks[14], (L, D_MODEL)),
        "w_xq": w(ks[15], (L, D_MODEL, D_MODEL), D_MODEL),
        "w_xkv": w(ks[16], (L, D_MODEL, 2 * D_MODEL), D_MODEL),
        "w_xo": w(ks[17], (L, D_MODEL, D_MODEL), D_MODEL),
        "g_ffn": gain(ks[18], (L, D_MODEL)),
        "w_up": w(ks[19], (L, D_MODEL, 2 * D_FF), D_MODEL),
        "w_conv": w(ks[20], (L, CONV_W, 2 * D_FF), CONV_W),
        "b_conv": 0.01 * jax.random.normal(ks[21], (L, 2 * D_FF), f32),
        "w_down": w(ks[22], (L, D_FF, D_MODEL), D_FF),
        "g_final": gain(ks[23], (D_MODEL,)),
    }

def reference(x, mem, positions, g_mix, w_in, b_gate, g_q_lat, w_uq, g_kv_lat, w_ukv, w_proj_mla,
              g_ret, w_proj_ret, w_out, g_cross, g_mem, w_xq, w_xkv, w_xo, g_ffn, w_up, w_conv,
              b_conv, w_down, g_final):
    B, S, D = x.shape
    M = mem.shape[1]
    sizes = (MLA_Q_RANK, MLA_KV_RANK, MLA_ROPE, RET_HEADS * RET_DK, RET_HEADS * RET_DK,
             RET_WIDTH, RET_WIDTH, 2 * D_MODEL)
    cuts = []
    acc = 0
    for sz in sizes[:-1]:
        acc += sz
        cuts.append(acc)
    h = x
    for l in range(DEPTH):
        u = rms_norm(h, g_mix[l])
        z = u @ w_in[l]
        c_q, c_kv, k_r, rq, rk, rv, rg, gates = jnp.split(z, cuts, axis=-1)

        q = (rms_norm(c_q, g_q_lat[l]) @ w_uq[l]).reshape(B, S, MLA_HEADS, MLA_NOPE + MLA_ROPE)
        q_nope, q_rope = q[..., :MLA_NOPE], rotary(q[..., MLA_NOPE:], positions)
        kv = (rms_norm(c_kv, g_kv_lat[l]) @ w_ukv[l]).reshape(B, S, MLA_HEADS, MLA_NOPE + MLA_V)
        k_nope, v_a = kv[..., :MLA_NOPE], kv[..., MLA_NOPE:]
        k_rope = jnp.broadcast_to(rotary(k_r[:, :, None, :], positions), (B, S, MLA_HEADS, MLA_ROPE))
        q_full = jnp.concatenate([q_nope, q_rope], axis=-1).transpose(0, 2, 1, 3)
        k_full = jnp.concatenate([k_nope, k_rope], axis=-1).transpose(0, 2, 1, 3)
        o_a = causal_block_attention(q_full, k_full, v_a.transpose(0, 2, 1, 3),
                                     (MLA_NOPE + MLA_ROPE) ** -0.5)
        y_a = o_a.transpose(0, 2, 1, 3).reshape(B, S, MLA_WIDTH) @ w_proj_mla[l]

        rq = rotary(rq.reshape(B, S, RET_HEADS, RET_DK), positions)
        rk = rotary(rk.reshape(B, S, RET_HEADS, RET_DK), positions) * (RET_DK ** -0.5)
        rv = rv.reshape(B, S, RET_HEADS, RET_DV)
        y_ret = head_group_norm(retention_chunkwise(rq, rk, rv), g_ret[l])
        y_r = (jax.nn.silu(rg) * y_ret) @ w_proj_ret[l]

        g_a, g_r = jnp.split(jax.nn.sigmoid(gates + b_gate[l]), 2, axis=-1)
        h = h + (g_a * y_a + g_r * y_r) @ w_out[l]

        xq = (rms_norm(h, g_cross[l]) @ w_xq[l]).reshape(B, S, X_HEADS, X_HEAD_DIM)
        mkv = (rms_norm(mem, g_mem[l]) @ w_xkv[l]).reshape(B, M, 2, X_HEADS, X_HEAD_DIM)
        mk, mv = mkv[:, :, 0], mkv[:, :, 1]
        s = jnp.einsum('bshd,bmhd->bhsm', xq, mk).astype(jnp.float32) * (X_HEAD_DIM ** -0.5)
        p = jax.nn.softmax(s, axis=-1).astype(mv.dtype)
        xo = jnp.einsum('bhsm,bmhd->bshd', p, mv).reshape(B, S, D)
        h = h + xo @ w_xo[l]

        up = causal_dwconv(rms_norm(h, g_ffn[l]) @ w_up[l], w_conv[l], b_conv[l])
        a, b = up[..., :D_FF], up[..., D_FF:]
        h = h + (jax.nn.silu(a) * b) @ w_down[l]
    return rms_norm(h, g_final)


_drawn_inputs = setup_inputs


def setup_inputs(seed=0):
    import zlib

    import numpy as np

    out = dict(_drawn_inputs(seed))
    spreads = {}
    factors = {'b_gate': 8.0,
     'g_q_lat': 8.0,
     'g_kv_lat': 8.0,
     'g_ret': 3.153,
     'g_cross': 8.0,
     'g_mem': 6.977,
     'b_conv': 51.949,
     'g_ffn': 8.0}
    for name, (base, spread) in spreads.items():
        noise = np.random.default_rng([zlib.crc32(name.encode()), seed]).standard_normal(out[name].shape)
        drawn = base * np.exp(spread * noise) if base else spread * noise
        out[name] = __import__('jax').numpy.asarray(drawn.astype(out[name].dtype))
    for name, factor in factors.items():
        out[name] = (out[name] * factor).astype(out[name].dtype)
    return out
```

```python
import numpy as np
import concourse.bass as bass
from concourse import mybir
from contextlib import ExitStack

D = 1024
T = 1024
P = 128
H2 = 512
KB = D // P
NT = T // P
CH = H2 // P
NMEM = 256
MB = NMEM // P
RH = 4
RDK = 128
MH = 8
NOPE, ROPE, DV = 64, 32, 64
QK = NOPE + ROPE
QR, KVR = 256, 128
QB = QR // P
XH, XD = 4, 256
FF = 2816
FB = FF // P
FGROUPS = (6, 6, 6, 4)
EPS = 1e-6
SLOTS = 4
RAWS = 2
XR = 3
PI = 3.1415925
TWO_PI_PARTS = (6.25, 0.033203125, -1.7821788787841797e-05, -5.2954e-10)

C_KV, C_KR = QR, QR + KVR
C_RQ = C_KR + ROPE
C_RK, C_RV, C_RG = C_RQ + RH * RDK, C_RQ + 2 * RH * RDK, C_RQ + 3 * RH * RDK
C_GA = C_RQ + 4 * RH * RDK
C_GR = C_GA + D


def starts(sizes):
    at, n = {}, 0
    for name, size in sizes:
        at[name] = n
        n += size
    return at, n


SLAB0, FF_SLAB0 = starts((("ret", 4 * RH), ("ga", KB), ("gr", 2 * KB), ("lat", 4), ("mla", 4), ("mix", KB // 2),
                          ("out", KB), ("xq", KB), ("xkv", 2 * KB), ("xo", KB)))
NSLAB = FF_SLAB0 + sum(2 * g + KB for g in FGROUPS)
assert NSLAB % SLOTS == 0 and all(v % SLOTS == 0 for v in SLAB0.values())
USE0, FF_USE0 = starts((("ret", 4 * RH), ("ga", KB), ("gr", 2 * KB), ("lat", 4), ("qrow", NT), ("vrow", NT // 2),
                        ("xt", NT), ("mix", KB), ("out", KB), ("xq", KB), ("xkv", KB), ("xa", 2 * XH), ("xo", KB)))
FIN_USE0 = FF_USE0 + sum(2 * g + KB for g in FGROUPS)
SMALL = (("g_mix", 8), ("g_cross", 8), ("g_ffn", 8), ("g_final", 8), ("g_mem", 8), ("b_gate", 16), ("g_q_lat", 2),
         ("g_kv_lat", 1), ("g_ret", 4), ("cw0", 44), ("cw1", 44), ("cw2", 44), ("b_conv", 44))
SM0, NSMALL = starts(SMALL)
R64, R16 = RDK // 2, ROPE // 2
NF = R64 + R16
CN0, NCONST = starts((("ident", 128), ("tri", 128), ("mask", 128), ("ones", 128), ("inv", NF), ("xi", RH),
                      ("zeta", RH), ("ginv", RH), ("gC", RH), ("eps", 1)))


def build(nc, x, mem, pos, slabs, small, const, out):
    f32, f32r, i32 = mybir.dt.float32, mybir.dt.float32r, mybir.dt.int32
    ALU, ACT, AX = mybir.AluOpType, mybir.ActivationFunctionType, mybir.AxisListType
    ds = bass.ds
    ctx = ExitStack()

    def place(kb, specs):
        with ExitStack() as st:
            if kb:
                st.enter_context(nc.sbuf_tensor(f"below_{specs[0][0]}", [P, int(kb * 256)], f32))
            return [st.enter_context(nc.sbuf_tensor(n, s, f32r if r else f32)) for n, s, r in specs]

    def at_least(eng, s, v):
        if not (isinstance(v, int) and v <= 0):
            eng.wait_ge(s, v)

    def apart(eng, *of):
        if not all(isinstance(v, int) for v in of):
            eng.nop(nofuse=True)

    with ctx:
        def sb(name, shape, dt=f32):
            return ctx.enter_context(nc.sbuf_tensor(name, shape, dt))

        def sem(name):
            return ctx.enter_context(nc.semaphore(name))

        raw = sb("raw", [P, RAWS, 1024])
        wh = sb("wh", [P, SLOTS, 1024], f32r)
        wl = sb("wl", [P, SLOTS, 1024], f32r)
        sm = sb("sm", [P, NSMALL])
        cn = sb("cn", [P, NCONST])
        ones_r = sb("ones_r", [P, P], f32r)
        ident_r = sb("ident_r", [P, P], f32r)
        mask_r = sb("mask_r", [P, P], f32r)
        posi = sb("posi", [P, NT], i32)
        posf = sb("posf", [P, NT])
        ssq = sb("ssq", [P, NT])
        rst_x = sb("rst_x", [P, NT])
        mst = sb("mst", [P, 3, MB])
        amax, aneg, asum, ainv = (sb(n, [P, 2, CH]) for n in ("amax", "aneg", "asum", "ainv"))
        ps = ctx.enter_context(nc.psum_tensor("ps", [P, 8, H2], f32))

        uh, ul = place(0, [("uh", [P, KB, T], 1), ("ul", [P, KB, T], 1)])
        xs, ang, kk, junk = place(64, [("xs", [P, NT, D], 0), ("ang", [P, NT, NF], 0), ("kk", [P, NT, NF], 0),
                                       ("junk", [P, D], 0)])
        yth, ytl = place(64, [("yth", [P, RH, T], 1), ("ytl", [P, RH, T], 1)])
        cosT, sinT = place(156.5, [("cosT", [P, NT, NF], 0), ("sinT", [P, NT, NF], 0)])
        (zq, zk, zv, sg, t1, t2, rq, rk, qth, qtl, kth, ktl, krh, krl, vh, vl, sh, sl, rst, rsh, rsl, yn, bns, mvv,
         rsd, t3, t4) = place(96, [(n, [P, T], 0) for n in ("zq", "zk", "zv", "sg")]
                      + [(n, [P, H2], 0) for n in ("t1", "t2", "rq", "rk")]
                      + [(n, [P, H2], 1) for n in ("qth", "qtl", "kth", "ktl", "krh", "krl", "vh", "vl", "sh", "sl")]
                      + [("rst", [P, CH + 1, P], 0), ("rsh", [P, H2], 1), ("rsl", [P, H2], 1), ("yn", [P, H2], 0),
                         ("bns", [P, CH, 6], 0), ("mvv", [P, CH, 2], 0), ("rsd", [P, 2, CH], 0), ("t3", [P, H2], 0), ("t4", [P, H2], 0)])
        (sig,) = place(96, [("sig", [P, 2, T], 0)])
        (mxr,) = place(112, [("mxr", [P, 2, T], 0)])
        cqh, cql, ckh, ckl, kbh, kbl, lz, lsq, lsh, lsl, lr, zkr, krow, kr1, kr2 = place(64, [
            ("cqh", [P, QB, T], 1), ("cql", [P, QB, T], 1), ("ckh", [P, T], 1), ("ckl", [P, T], 1),
            ("kbh", [P, 2, T], 1), ("kbl", [P, 2, T], 1),
            ("lz", [P, 3, T], 0), ("lsq", [P, H2], 0), ("lsh", [P, H2], 1), ("lsl", [P, H2], 1), ("lr", [P, 2, T], 0),
            ("zkr", [ROPE, T], 0), ("krow", [P, NT, QK], 0), ("kr1", [P, NT, ROPE], 0),
            ("kr2", [P, NT, ROPE], 0)])
        vrh, vrl, qrow, qr1, qr2 = place(0, [("vrh", [P, NT, MH * DV], 1), ("vrl", [P, NT, MH * DV], 1),
                                             ("qrow", [P, NT, MH * QK], 0), ("qr1", [P, MH, ROPE], 0),
                                             ("qr2", [P, MH, ROPE], 0)])
        mqh, mql = place(64, [("mqh", [P, 2, T], 1), ("mql", [P, 2, T], 1)])
        orow, prow, pth, ptl = place(104, [("orow", [P, NT, MH * DV], 0), ("prow", [P, 2, T], 0),
                                           ("pth", [P, 2, T], 1), ("ptl", [P, 2, T], 1)])
        oth, otl = place(32, [("oth", [P, RH, T], 1), ("otl", [P, RH, T], 1)])
        (xtile,) = place(144, [("xtile", [P, XR, D], 0)])
        (hT,) = place(0, [("hT", [P, KB, T], 0)])
        mih, mil, sab, mrb = place(64, [("mih", [P, KB, T], 1), ("mil", [P, KB, T], 1), ("sab", [P, 2, T], 0),
                                        ("mrb", [P, 2, T], 0)])
        g0h, g0l, g1h, g1l = place(32, [("g0h", [P, KB, H2], 1), ("g0l", [P, KB, H2], 1),
                                        ("g1h", [P, KB, H2], 1), ("g1l", [P, KB, H2], 1)])
        acc, rbc, sq, ach, acl = place(128, [("acc", [P, 2, H2], 0), ("rbc", [P, 2, H2], 0), ("sq", [P, 2, H2], 0),
                                             ("ach", [P, 2, H2], 1), ("acl", [P, 2, H2], 1)])
        (xqh,) = place(0, [("xqh", [P, KB, T], 1)])
        (xql,) = place(96, [("xql", [P, KB, T], 1)])
        xf, mrow = place(148, [("xf", [P, 2, H2], 0), ("mrow", [P, MB, D], 0)])
        mkh, mkl, mvh, mvl = place(32, [("mkh", [P, KB, NMEM], 1), ("mkl", [P, KB, NMEM], 1),
                                        ("mvh", [P, MB, D], 1), ("mvl", [P, MB, D], 1)])
        mth, mtl, vT = place(64, [("mth", [P, KB, NMEM], 1), ("mtl", [P, KB, NMEM], 1),
                                  ("vT", [P, 2, NMEM], 0)])
        pr, xph, xpl = place(64, [("pr", [P, 2, CH, NMEM], 0), ("xph", [P, 2, MB * H2], 1),
                                  ("xpl", [P, 2, MB * H2], 1)])
        (hF,) = place(32, [("hF", [P, KB, T], 0)])
        f0h, f0l = place(64, [("f0h", [P, KB, H2], 1), ("f0l", [P, KB, H2], 1)])
        f1h, f1l = place(0, [("f1h", [P, KB, H2], 1), ("f1l", [P, KB, H2], 1)])
        (hs,) = place(148, [("hs", [P, 2, T], 0)])
        (rbF,) = place(157, [("rbF", [P, 2, H2], 0)])
        fah, fal, z, ya, yb = place(96, [("fah", [P, 6, T], 1), ("fal", [P, 6, T], 1), ("z", [P, T + 2], 0),
                                         ("ya", [P, T], 0), ("yb", [P, T], 0)])
        (yo,) = place(0, [("yo", [P, KB, T], 0)])
        acc2, sq2, ach2, acl2, orows, rs8 = place(64, [
            ("acc2", [P, 2, H2], 0), ("sq2", [P, 2, H2], 0), ("ach2", [P, 2, H2], 1), ("acl2", [P, 2, H2], 1),
            ("orows", [P, 2, D], 0), ("rs8", [P, NT, 2], 0)])

        ident = cn[:, CN0["ident"]:CN0["ident"] + P]
        tri = cn[:, CN0["tri"]:CN0["tri"] + P]

        def col(t, at, i):
            return t[:, at + i:at + i + 1] if isinstance(i, int) else t[:, ds(at + i, 1)]

        def smc(name, i=0):
            return col(sm, SM0[name], i)

        def cnc(name, i=0):
            return col(cn, CN0[name], i)

        def blk(t, i, lo=0, hi=T):
            return t[:, i, lo:hi] if isinstance(i, int) else t[:, ds(i, 1), lo:hi].rearrange("p a n -> p (a n)")

        def half(b):
            return slice(b * H2, (b + 1) * H2)

        s_ga = nc.dram_tensor("s_ga", (KB, P, T), f32, kind="Internal").ap()
        s_mr = nc.dram_tensor("s_mr", (KB, P, T), f32, kind="Internal").ap()
        s_h = nc.dram_tensor("s_h", (KB, P, T), f32, kind="Internal").ap()

        def row(t, i):
            return t[i] if isinstance(i, int) else t[ds(i, 1)].rearrange("a p n -> (a p) n")

        S = {}
        for name in ("ld0 ld1 w_hi w_ready w_used par done0 done1 free0 free1 "
                     "x_ld0 x_ld1 x_ld2 x_ld3 x_ld4 x_ld5 x_ld6 x_ld7 x_sq x_std x_rs x_row xT_t xT_hi xT_lo "
                     "cst angs sinr sins "
                     "rows_qk rot_t rot t_qk qk_hi qk_lo kr_hi kr_lo rows_v v_hi v_lo s_t s_m s_hi s_lo kv_t r_st gn_rc "
                     "r_hi r_lo y_t gn_st var std yn_done yT_t yg_done y_hi y_lo "
                     "g_st0 g_st1 m_st0 m_st1 "
                     "l_sq l_sh l_sl l_ss l_std l_rc l_c l_hi l_lo k_row k_r1 k_r2 k_T k_hi k_lo "
                     "q_r1 q_rope v_evh aux_t aux_hi aux_lo m_s m_mx m_neg m_exp m_ptt m_pth m_ptl "
                     "m_pv m_ri m_o xt_ld0 xt_ld1 xt_ld2 sa_ld0 sa_ld1 mr_ld0 mr_ld1 mix_m mix_hi mix_lo "
                     "o_gh o_gl o_sq o_ac o_z ac_h ac_l ss_t ss_s rb_r g1_h g1_l h_sp "
                     "xq_h xq_l mm_ld mm_sq mm_st mm_rc mm_n mm_t mm_hi mm_lo kv_h vT_t mv_h mv_l "
                     "xa_s xa_m xa_n xa_e xa_r xa_p xa_t xa_h xa_l xo_h hs_ld0 hs_ld1 "
                     "c_y0 c_y c_s c_g c_hi c_lo c_zp o_y out_st0 out_st1").split():
            S[name] = sem(name)
        d_done, d_free = (S["done0"], S["done1"]), (S["free0"], S["free1"])

        block = ctx.enter_context(nc.Block())

        @block.sync
        def _(sp):
            for t in range(NT):
                sp.dma_start(xs[:, t, :], x[t * P:(t + 1) * P, :]).then_inc(S[f"x_ld{t}"], 16)
                if t == CH - 1:
                    sp.dma_start(cn[:, :], const).then_inc(S["par"], 16)
                    sp.dma_start(sm[:, :], small).then_inc(S["par"], 16)
                    sp.dma_start(posi[:, :], pos).then_inc(S["par"], 16)
                    for j in range(RAWS):
                        sp.dma_start(raw[:, j, :], slabs[j]).then_inc(S[f"ld{j}"], 16)
            for j in range(RAWS, SLOTS):
                sp.wait_ge(S["w_ready"], j - RAWS + 1)
                sp.dma_start(raw[:, j % RAWS, :], slabs[j]).then_inc(S[f"ld{j % RAWS}"], 16)
            with sp.Fori(1, NSLAB // SLOTS) as i:
                for j in range(SLOTS):
                    sp.wait_ge(S["w_ready"], SLOTS * i + (j - RAWS + 1))
                    sp.dma_start(raw[:, j % RAWS, :], row(slabs, SLOTS * i + j)).then_inc(S[f"ld{j % RAWS}"], 16)

        @block.gpsimd
        def _(pool):
            def split(i, j):
                s = SLOTS * i + j
                pool.wait_ge(S[f"ld{j % RAWS}"], 16 * (SLOTS // RAWS * i + j // RAWS + 1))
                if not isinstance(i, int) or i > 0:
                    pool.wait_ge(S["w_used"], SLOTS * (i - 1) + j + 1)
                apart(pool, i)
                pool.tensor_scalar(wh[:, j, :], raw[:, j % RAWS, :], 1.0, None, ALU.mult).then_inc(S["w_hi"], 1)
                pool.wait_ge(S["w_hi"], s + 1)
                pool.tensor_tensor(wl[:, j, :], raw[:, j % RAWS, :], wh[:, j, :].bitcast(f32),
                                   ALU.subtract).then_inc(S["w_ready"], 1)
            for j in range(SLOTS):
                split(0, j)
            with pool.Fori(1, NSLAB // SLOTS) as i:
                for j in range(SLOTS):
                    split(i, j)

        @block.tensor
        def _(pe):
            def mm3(o, lh, ll, rh, rl, start, stop, freed=0, extra=None):
                l = pe.matmul(o, lh, rh, start=start, stop=False)
                if freed:
                    l.then_inc(S["w_used"], freed)
                if extra:
                    extra()
                pe.matmul(o, lh, rl, start=False, stop=False)
                return pe.matmul(o, ll, rh, start=False, stop=stop)

            def wslot(j, k, n=P, at=0, width=None):
                c = k * (width or n) + at
                return wh[:, j, c:c + n], wl[:, j, c:c + n]

            def dense(j, s, u, nk, act, width=P, at=0, m=P, freed=1, first=True, between=(None, None)):
                if first:
                    pe.wait_ge(S["w_ready"], s + 1)
                for b in range(2):
                    at_least(pe, d_free[b], u)
                    for k in range(nk):
                        l = mm3(ps[0:m, b, :], *wslot(j, k, m, at, width), *act(k, b), k == 0, k == nk - 1,
                                freed if first and b == k == 0 else 0)
                    l.then_inc(d_done[b], 1)
                    if between[b]:
                        between[b]()

            def of(h, l):
                return lambda k, b: (h[:, k, half(b)], l[:, k, half(b)])

            pe.wait_ge(S["par"], 48)
            for n in range(2 * KB):
                b, k = n // KB, n % KB
                if k == 0:
                    pe.wait_ge(S["x_row"], CH * (b + 1))
                if n >= 6:
                    pe.wait_ge(S["xT_lo"], n - 5)
                for j in range(CH):
                    l = pe.transpose(ps[:, 2 + n % 6, j * P:(j + 1) * P], xs[:, CH * b + j, k * P:(k + 1) * P], ident)
                l.then_inc(S["xT_t"], 1)

            def rows_qk(h, u):
                w = 2 * h + u
                pe.wait_ge(d_free[u], 4 * h + 2)
                at_least(pe, S["qk_lo"], w)
                for bank, zz in ((2, zq), (3, zk)):
                    for j in range(CH):
                        c = u * H2 + j * P
                        l = pe.transpose(ps[:, bank, j * P:(j + 1) * P], zz[:, c:c + P], ident)
                l.then_inc(S["rows_qk"], 1)

            def back_qk(h, u):
                pe.wait_ge(S["rot"], 2 * h + u + 1)
                for bank, rr in ((2, rq), (3, rk)):
                    for j in range(CH):
                        l = pe.transpose(ps[:, bank, j * P:(j + 1) * P], rr[:, j * P:(j + 1) * P], ident)
                l.then_inc(S["t_qk"], 1)

            def rows_v(h, u):
                pe.wait_ge(d_free[u], 4 * h + 3)
                at_least(pe, S["r_st"], (CH + 1) * (2 * h + u))
                for j in range(CH):
                    c = u * H2 + j * P
                    l = pe.transpose(ps[:, 4, j * P:(j + 1) * P], zv[:, c:c + P], ident)
                l.then_inc(S["rows_v"], 1)

            def scores(h, u):
                w = 2 * h + u
                pe.wait_ge(S["qk_lo"], w + 1)
                at_least(pe, S["s_m"], w)
                for j in range(CH):
                    c = slice(j * P, (j + 1) * P)
                    l = mm3(ps[:, 5, c], kth[:, c], ktl[:, c], qth[:, c], qtl[:, c], True, True)
                l.then_inc(S["s_t"], 1)

            def states(h, u):
                w = 2 * h + u
                pe.wait_ge(S["kr_lo"], w + 1)
                pe.wait_ge(S["v_lo"], w + 1)
                for j in range(CH):
                    c = slice(j * P, (j + 1) * P)
                    l = mm3(ps[:, 4, c], krh[:, c], krl[:, c], vh[:, c], vl[:, c], True, True)
                l.then_inc(S["kv_t"], 1)

            def outs(h, u):
                w = 2 * h + u
                pe.wait_ge(S["s_lo"], w + 1)
                pe.wait_ge(S["r_lo"], w + 1)
                at_least(pe, S["yn_done"], w)
                for j in range(CH):
                    c = slice(j * P, (j + 1) * P)
                    mm3(ps[:, 6, c], sh[:, c], sl[:, c], vh[:, c], vl[:, c], True, False)
                    l = mm3(ps[:, 6, c], qth[:, c], qtl[:, c], rsh[:, c], rsl[:, c], False, True)
                l.then_inc(S["y_t"], 1)

            def back_y(h, u):
                w = 2 * h + u
                pe.wait_ge(S["yn_done"], w + 1)
                at_least(pe, S["yg_done"], w)
                for j in range(CH):
                    l = pe.transpose(ps[:, 7, j * P:(j + 1) * P], yn[:, j * P:(j + 1) * P], ident)
                l.then_inc(S["yT_t"], 1)

            def between(h, last=False):
                first = isinstance(h, int) and h == 0
                old = (lambda f, u: None) if first else (lambda f, u: f(h - 1, u))
                new = (lambda f, u: None) if last else (lambda f, u: f(h, u))
                return (
                    (lambda: (old(back_y, 0), old(back_qk, 1)), lambda: (old(rows_v, 1), old(scores, 1))),
                    (lambda: old(states, 1), lambda: (old(outs, 1), new(rows_qk, 0))),
                    (lambda: (old(back_y, 1), new(back_qk, 0)), lambda: (new(rows_v, 0), new(scores, 0))),
                    (lambda: (new(states, 0), new(rows_qk, 1)), lambda: new(outs, 0)))

            pe.wait_ge(S["xT_lo"], 2 * KB)
            for j, pair in enumerate(between(0)):
                dense(j, j, j, KB, of(uh, ul), between=pair, freed=int(j > 0))
            with pe.Fori(1, RH) as h:
                for j, pair in enumerate(between(h)):
                    dense(j, 4 * h + j, 4 * h + j, KB, of(uh, ul), between=pair)

            for j, pair in enumerate(between(RH, last=True)):
                dense(j, SLAB0["ga"] + j, USE0["ga"] + j, KB, of(uh, ul), between=pair)
            with pe.Fori(1, KB // 4) as i:
                for j in range(4):
                    dense(j, SLAB0["ga"] + 4 * i + j, USE0["ga"] + 4 * i + j, KB, of(uh, ul))

            pe.wait_ge(S["y_lo"], 2 * RH)
            with pe.Fori(0, KB // 2) as i:
                for j in range(4):
                    s, u = SLAB0["gr"] + 4 * i + j, USE0["gr"] + 4 * i + j
                    if j % 2 == 0:
                        dense(j, s, u, KB, of(uh, ul))
                    else:
                        dense(j, s, u, RH, of(yth, ytl))

            for j in range(4):
                dense(j, SLAB0["lat"] + j, USE0["lat"] + j, KB, of(uh, ul), m=(ROPE if j == 3 else P),
                      width=(ROPE if j == 3 else P))
            pe.wait_ge(d_free[1], USE0["lat"] + 4)
            for t in range(NT):
                l = pe.transpose(ps[:, 7, t * ROPE:(t + 1) * ROPE], zkr[:, t * P:(t + 1) * P], ident[0:ROPE, 0:ROPE])
            l.then_inc(S["k_row"], 1)
            for n, (bank, f, l_) in enumerate(((2, True, False), (2, False, True), (4, True, True),
                                               (3, True, False), (3, False, True), (5, True, True))):
                pe.wait_ge(S["l_sl"], n + 1)
                pe.matmul(ps[:, bank, :], ones_r[:, :], lsh[:, :], start=f, stop=False)
                pe.matmul(ps[:, bank, :], ones_r[:, :], lsl[:, :], start=False, stop=l_).then_inc(S["l_ss"], 1)
            pe.wait_ge(S["k_r2"], 3)
            for b in range(2):
                for j in range(CH):
                    l = pe.transpose(ps[0:QK, 6 + b, j * P:(j + 1) * P], krow[:, CH * b + j, :], ident)
                l.then_inc(S["k_T"], 1)

            for j in range(QB):
                pe.wait_ge(S["w_ready"], SLAB0["mla"] + j + 1)
            pe.wait_ge(S["l_lo"], 6)
            HW = MH // 2 * QK
            for t in range(NT):
                for b in range(2):
                    pe.wait_ge(d_free[b], USE0["qrow"] + t)
                    for k in range(QB):
                        l = mm3(ps[:, b, 0:HW], cqh[:, k, t * P:(t + 1) * P], cql[:, k, t * P:(t + 1) * P],
                                wh[:, k, b * HW:(b + 1) * HW], wl[:, k, b * HW:(b + 1) * HW], k == 0, k == QB - 1,
                                freed=int(t == b == k == 0))
                    l.then_inc(d_done[b], 1)
            for j in range(2):
                pe.wait_ge(S["w_ready"], SLAB0["mla"] + QB + j + 1)
            for t in range(NT):
                b = t % 2
                pe.wait_ge(d_free[b], USE0["vrow"] + t // 2)
                l = mm3(ps[:, b, :], ckh[:, t * P:(t + 1) * P], ckl[:, t * P:(t + 1) * P], wh[:, 3, 0:MH * DV],
                        wl[:, 3, 0:MH * DV], True, True, freed=(QB if t == 0 else 0))
                l.then_inc(d_done[b], 1)

            def aux(h, n):
                x_ = 4 * h + n
                if x_ == 0:
                    pe.wait_ge(d_free[0], USE0["vrow"] + NT // 2)
                else:
                    pe.wait_ge(S["aux_lo"], x_)
                b = n % 2
                if n < 2:
                    l = mm3(ps[0:NOPE, 0, :], wh[:, 2, h * NOPE:(h + 1) * NOPE], wl[:, 2, h * NOPE:(h + 1) * NOPE],
                            ckh[:, half(b)], ckl[:, half(b)], True, True)
                else:
                    if h == 0 and n == 2:
                        pe.wait_ge(S["q_rope"], NT)
                    for j in range(CH):
                        l = pe.transpose(ps[0:QK, 0, j * P:(j + 1) * P], qrow[:, CH * b + j, h * QK:(h + 1) * QK],
                                         ident)
                        if (h, n, j) == (MH - 1, 2, 0):
                            l.then_inc(S["w_used"], 2)
                l.then_inc(S["aux_t"], 1)

            def aux_o(fb, b):
                x_ = 4 * MH + 2 * fb + b
                pe.wait_ge(S["aux_lo"], x_)
                pe.wait_ge(S["m_o"], NT * (2 * fb + 2))
                for j in range(CH):
                    l = pe.transpose(ps[:, 0, j * P:(j + 1) * P], orow[:, CH * b + j, fb * P:(fb + 1) * P], ident)
                l.then_inc(S["aux_t"], 1)

            def m_scores(w):
                h, i = divmod(w, NT)
                at_least(pe, S["m_exp"], w - 1)
                if i == 0:
                    pe.wait_ge(S["aux_lo"], 4 * h + 4)
                    if h == 0:
                        pe.wait_ge(S["k_lo"], 4)
                p = h % 2
                q = slice(i * P, (i + 1) * P)
                for c in range(i // CH + 1):
                    n = min(CH, i + 1 - c * CH) * P
                    bank = 2 + 2 * (w % 2) + c
                    diag = c == i // CH
                    keys = slice(c * H2, c * H2 + n)

                    def mask(o=ps[:, bank, n - P:n]):
                        pe.matmul(o, ident_r[:, :], mask_r[:, :], start=False, stop=False, skip_group_check=True)
                    l = mm3(ps[:, bank, 0:n], mqh[0:QK, p, q], mql[0:QK, p, q], kbh[0:QK, p, keys], kbl[0:QK, p, keys],
                            True, True, extra=mask if diag else None)
                l.then_inc(S["m_s"], 1)

            def m_turn(w):
                h, i = divmod(w, NT)
                pe.wait_ge(S["m_exp"], w + 1)
                at_least(pe, S["m_ptl"], w)
                for c in range(i + 1):
                    l = pe.transpose(ps[:, 6 + c // CH, (c % CH) * P:(c % CH + 1) * P],
                                     prow[:, w % 2, c * P:(c + 1) * P], ident)
                l.then_inc(S["m_ptt"], 1)

            def m_pv(w):
                h, i = divmod(w, NT)
                pe.wait_ge(S["m_ptl"], w + 1)
                if w == 0:
                    for b in range(2):
                        pe.wait_ge(d_free[b], USE0["vrow"] + NT // 2)
                else:
                    pe.wait_ge(S["m_o"], w)
                for c in range(i + 1):
                    v = slice(h * DV, (h + 1) * DV)
                    l = mm3(ps[:, 1, 0:DV], pth[:, w % 2, c * P:(c + 1) * P], ptl[:, w % 2, c * P:(c + 1) * P],
                            vrh[:, c, v], vrl[:, c, v], c == 0, c == i)
                l.then_inc(S["m_pv"], 1)

            for n in range(4):
                aux(0, n)
            NW = MH * NT
            m_scores(0)
            for w in range(NW):
                h, i = divmod(w, NT)
                if w + 1 < NW:
                    m_scores(w + 1)
                m_turn(w)
                if w:
                    m_pv(w - 1)
                if 1 <= i <= 4 and h + 1 < MH:
                    aux(h + 1, i - 1)
                if h == MH - 1 and 1 <= i <= 6:
                    aux_o((i - 1) // 2, (i - 1) % 2)
            m_pv(NW - 1)

            for t in range(NT):
                pe.wait_ge(S[f"xt_ld{t % XR}"], 16 * (t // XR + 1))
                for b in range(2):
                    if t == 0:
                        pe.wait_ge(S["aux_lo"], 4 * MH + 6) if b == 0 else pe.wait_ge(S["m_o"], NW)
                    else:
                        pe.wait_ge(d_free[b], USE0["xt"] + t)
                    for j in range(CH):
                        k = CH * b + j
                        l = pe.transpose(ps[:, b, j * P:(j + 1) * P], xtile[:, t % XR, k * P:(k + 1) * P], ident)
                    l.then_inc(d_done[b], 1)
                if t == 1:
                    for b in range(2):
                        if b == 0:
                            pe.wait_ge(S["m_o"], NW)
                        for j in range(CH):
                            l = pe.transpose(ps[:, 2 + b, j * P:(j + 1) * P], orow[:, CH * b + j, 3 * P:4 * P], ident)
                        l.then_inc(S["aux_t"], 1)

            pe.wait_ge(S["aux_lo"], 4 * MH + 8)
            for j in range(KB // 2):
                for m in range(2):
                    dense(j, SLAB0["mix"] + j, USE0["mix"] + 2 * j + m, RH, of(oth, otl), width=2 * P, at=m * P,
                          first=(m == 0), freed=int(j > 0))

            pe.wait_ge(S["mix_lo"], 2 * KB)
            with pe.Fori(0, KB // 4) as i:
                for j in range(4):
                    dense(j, SLAB0["out"] + 4 * i + j, USE0["out"] + 4 * i + j, KB, of(mih, mil))

            def sums(n):
                pe.wait_ge(S["ac_l"], n + 1)
                for b in range(2):
                    pe.matmul(ps[:, 2 + b, :], ones_r[:, :], ach[:, b, :], start=True, stop=False)
                    l = pe.matmul(ps[:, 2 + b, :], ones_r[:, :], acl[:, b, :], start=False, stop=True)
                l.then_inc(S["ss_t"], 1)

            def halves(h0, l0, h1, l1):
                return lambda k, b: (h0[:, k, :], l0[:, k, :]) if b == 0 else (h1[:, k, :], l1[:, k, :])

            pe.wait_ge(S["o_gl"], KB)
            dense(0, SLAB0["xq"], USE0["xq"], KB, halves(g0h, g0l, g1h, g1l),
                  between=(lambda: (sums(0), pe.wait_ge(S["g1_l"], KB)), None))
            for j in range(1, 4):
                dense(j, SLAB0["xq"] + j, USE0["xq"] + j, KB, halves(g0h, g0l, g1h, g1l))
            with pe.Fori(1, KB // 4) as i:
                for j in range(4):
                    dense(j, SLAB0["xq"] + 4 * i + j, USE0["xq"] + 4 * i + j, KB, halves(g0h, g0l, g1h, g1l))

            pe.wait_ge(S["mm_n"], MB)
            for n in range(KB // 2):
                for k in range(2):
                    for r in range(MB):
                        l = pe.transpose(ps[:, 4 + n, (2 * k + r) * P:(2 * k + r + 1) * P],
                                         mrow[:, r, (2 * n + k) * P:(2 * n + k + 1) * P], ident)
                l.then_inc(S["mm_t"], 1)
            pe.wait_ge(S["mm_lo"], KB)

            def mem_out(i, j, base):
                s = SLAB0["xkv"] + base + 4 * i + j
                b = j % 2
                pe.wait_ge(S["w_ready"], s + 1)
                pe.wait_ge(d_free[b], USE0["xkv"] + base // 2 + 2 * i + j // 2)
                for k in range(KB):
                    l = mm3(ps[:, b, 0:NMEM], *wslot(j, k), mth[:, k, :], mtl[:, k, :], k == 0, k == KB - 1,
                            freed=int(k == 0))
                l.then_inc(d_done[b], 1)

            with pe.Fori(0, 2) as i:
                for j in range(4):
                    mem_out(i, j, 0)

            def value_rows(m, b):
                pe.wait_ge(d_free[b], USE0["xkv"] + (KB + m) // 2 + 1)
                at_least(pe, S["mv_l"], m)
                for r in range(MB):
                    l = pe.transpose(ps[:, 4, r * P:(r + 1) * P], vT[:, b, r * P:(r + 1) * P], ident)
                l.then_inc(S["vT_t"], 1)
            for i in range(2):
                for j in range(4):
                    mem_out(i, j, KB)
                    m = 4 * i + j
                    if m:
                        value_rows(m - 1, (m - 1) % 2)
            def xa_s(v):
                j, b = divmod(v, 2)
                at_least(pe, S["xa_e"], v - 1)
                for t in range(CH):
                    bank = 2 + t // 2 if v % 2 == 0 else 4 + t // 2
                    c = (t % 2) * NMEM
                    q = slice(b * H2 + t * P, b * H2 + (t + 1) * P)
                    for k in range(2):
                        l = mm3(ps[:, bank, c:c + NMEM], xqh[:, 2 * j + k, q], xql[:, 2 * j + k, q],
                                mkh[:, 2 * j + k, :], mkl[:, 2 * j + k, :], k == 0, k == 1)
                l.then_inc(S["xa_s"], 1)

            def xa_t(v):
                pe.wait_ge(S["xa_p"], v + 1)
                at_least(pe, S["xa_l"], v)
                for k in range(MB):
                    for t in range(CH):
                        l = pe.transpose(ps[:, 6 + k, t * P:(t + 1) * P], pr[:, v % 2, t, k * P:(k + 1) * P], ident)
                l.then_inc(S["xa_t"], 1)

            def xa_pv(v):
                j = v // 2
                pe.wait_ge(S["xa_l"], v + 1)
                if v == 0:
                    pe.wait_ge(S["mv_l"], KB)
                for b in range(2):
                    pe.wait_ge(d_free[b], USE0["xa"] + v)
                    for k in range(MB):
                        c = slice(j * XD + b * P, j * XD + (b + 1) * P)
                        l = mm3(ps[:, b, :], mvh[:, k, c], mvl[:, k, c], xph[:, v % 2, k * H2:(k + 1) * H2],
                                xpl[:, v % 2, k * H2:(k + 1) * H2], k == 0, k == MB - 1)
                    l.then_inc(d_done[b], 1)

            pe.wait_ge(S["xq_l"], 2 * KB)
            for b in range(2):
                pe.wait_ge(d_free[b], USE0["xkv"] + KB)
            xa_s(0)
            value_rows(KB - 1, (KB - 1) % 2)
            pe.wait_ge(S["mv_l"], KB)
            for v in range(2 * XH):
                if v + 1 < 2 * XH:
                    xa_s(v + 1)
                xa_t(v)
                if v:
                    xa_pv(v - 1)
            xa_pv(2 * XH - 1)

            for b in range(2):
                pe.wait_ge(d_free[b], USE0["xo"])
            with pe.Fori(0, KB // 4) as i:
                for j in range(4):
                    dense(j, SLAB0["xo"] + 4 * i + j, USE0["xo"] + 4 * i + j, KB, of(xqh, xql))

            s, u, blocks = FF_SLAB0, FF_USE0, 0
            for g, G in enumerate(FGROUPS):
                n0 = 0
                if g == 0:
                    pe.wait_ge(S["o_gl"], 2 * KB)
                    dense(0, s, u, KB, halves(f0h, f0l, f1h, f1l),
                          between=(lambda: (sums(1), pe.wait_ge(S["g1_l"], 2 * KB)), None))
                    for j in range(1, 4):
                        dense(j, s + j, u + j, KB, halves(f0h, f0l, f1h, f1l))
                    n0 = 1
                with pe.Fori(n0, G // 2) as i:
                    for j in range(4):
                        dense(j, s + 4 * i + j, u + 4 * i + j, KB, halves(f0h, f0l, f1h, f1l))
                s, u, blocks = s + 2 * G, u + 2 * G, blocks + G
                pe.wait_ge(S["c_lo"], 2 * blocks)
                with pe.Fori(0, KB // 4) as i:
                    for j in range(4):
                        dense(j, s + 4 * i + j, u + 4 * i + j, G, of(fah, fal))
                s, u = s + KB, u + KB
            pe.wait_ge(S["o_y"], 2 * KB)
            for t in range(NT):
                for b in range(2):
                    pe.wait_ge(d_free[b], FIN_USE0 + t)
                    for j in range(CH):
                        l = pe.transpose(ps[:, b, j * P:(j + 1) * P], yo[:, CH * b + j, t * P:(t + 1) * P], ident)
                    l.then_inc(d_done[b], 1)
                if t == 0:
                    pe.wait_ge(S["ac_l"], 3)
                    for r in range(NT):
                        b, c = r // CH, slice(r % CH * P, (r % CH + 1) * P)
                        pe.matmul(ps[:, 2, 2 * r:2 * r + 2], ach2[:, b, c], ones_r[:, 0:2], start=True, stop=False)
                        l = pe.matmul(ps[:, 2, 2 * r:2 * r + 2], acl2[:, b, c], ones_r[:, 0:2], start=False,
                                      stop=True)
                    l.then_inc(S["ss_t"], 1)

        @block.scalar
        def _(act):
            def copy(o, i, **kw):
                return act.activation(o, i, ACT.Copy, **kw)

            for t in range(NT):
                act.wait_ge(S[f"x_ld{t}"], 16)
                at_least(act, S["x_sq"], t)
                act.activation(junk[:, :], xs[:, t, :], ACT.Square, accum_out=ssq[:, t:t + 1]).then_inc(S["x_sq"], 1)
                if t % CH == CH - 1:
                    b = t // CH
                    act.wait_ge(S["x_sq"], t + 1)
                    if b == 0:
                        act.wait_ge(S["par"], 48)
                    act.activation(rst_x[:, CH * b:CH * (b + 1)], ssq[:, CH * b:CH * (b + 1)], ACT.Sqrt,
                                   scale=1.0 / D, bias=cnc("eps")).then_inc(S["x_std"], 1)
            for n in range(2 * KB):
                b, k = n // KB, n % KB
                act.wait_ge(S["xT_t"], n + 1)
                copy(uh[:, k, half(b)], ps[:, 2 + n % 6, :], scale=smc("g_mix", k)).then_inc(S["xT_hi"], 1)
            act.wait_ge(S["angs"], 9)
            act.activation(sinT[:, :, :], ang[:, :, :], ACT.Sin).then_inc(S["sins"], 1)
            act.activation(cosT[:, :, :], kk[:, :, :], ACT.Sin).then_inc(S["sins"], 1)
            act.wait_ge(S["sins"], 2)

            def evac(h, j, b):
                act.wait_ge(d_done[b], 4 * h + j + 1)
                if j == 3:
                    at_least(act, S["yg_done"], 2 * h + b - 1)
                    act.activation(sg[:, half(b)], ps[:, b, :], ACT.Silu).then_inc(d_free[b], 1)
                else:
                    copy((zq, zk, zv)[j][:, half(b)], ps[:, b, :]).then_inc(d_free[b], 1)

            def kr_hi(h, u):
                act.wait_ge(S["rot"], 2 * h + u + 1)
                copy(krh[:, :], rk[:, :]).then_inc(S["kr_hi"], 1)

            def qk_hi(h, u):
                act.wait_ge(S["t_qk"], 2 * h + u + 1)
                copy(qth[:, :], ps[:, 2, :])
                copy(kth[:, :], ps[:, 3, :]).then_inc(S["qk_hi"], 1)

            def v_hi(h, u):
                act.wait_ge(S["rows_v"], 2 * h + u + 1)
                copy(vh[:, :], ps[:, 4, :]).then_inc(S["v_hi"], 1)

            def s_hi(h, u):
                act.wait_ge(S["s_m"], 2 * h + u + 1)
                copy(sh[:, :], t2[:, :]).then_inc(S["s_hi"], 1)

            def r_hi(h, u):
                act.wait_ge(S["r_st"], (CH + 1) * (2 * h + u + 1))
                copy(rsh[:, :], rst[:, 0:CH, :].rearrange("p a n -> p (a n)")).then_inc(S["r_hi"], 1)

            def y_std(h, u):
                act.wait_ge(S["var"], 2 * h + u + 1)
                act.activation(rsd[:, 0, :], mvv[:, :, 1], ACT.Sqrt, bias=cnc("eps")).then_inc(S["std"], 1)

            def y_hi(h, u):
                act.wait_ge(S["yg_done"], 2 * h + u + 1)
                apart(act, h)
                copy(blk(yth, h, u * H2, (u + 1) * H2), t1[:, :]).then_inc(S["y_hi"], 1)

            def order(h, ev, last=False):
                old = (lambda f, u: None) if isinstance(h, int) and h == 0 else (lambda f, u: f(h - 1, u))
                new = (lambda f, u: None) if last else (lambda f, u: f(h, u))
                ev(0, 0)
                old(y_hi, 0)
                old(qk_hi, 1)
                ev(0, 1)
                old(v_hi, 1)
                old(s_hi, 1)
                ev(1, 0)
                old(r_hi, 1)
                ev(1, 1)
                old(y_std, 1)
                new(kr_hi, 0)
                ev(2, 0)
                old(y_hi, 1)
                new(qk_hi, 0)
                ev(2, 1)
                new(v_hi, 0)
                new(s_hi, 0)
                ev(3, 0)
                new(r_hi, 0)
                new(kr_hi, 1)
                ev(3, 1)
                new(y_std, 0)

            order(0, lambda j, b: evac(0, j, b))
            with act.Fori(1, RH) as h:
                order(h, lambda j, b: evac(h, j, b))

            def gate_a(m, b, p):
                act.wait_ge(d_done[b], USE0["ga"] + m + 1)
                if b == 0 and m >= 2:
                    act.wait_ge(S[f"g_st{p}"], 16 * (m // 2))
                act.activation(sig[:, p, half(b)], ps[:, b, :], ACT.Sigmoid,
                               bias=smc("b_gate", m)).then_inc(d_free[b], 1)
                if b == 1:
                    for c in range(2):
                        act.wait_ge(d_free[c], USE0["ga"] + m + 1)
                    act.dma_start(row(s_ga, m), sig[:, p, :]).then_inc(S[f"g_st{p}"], 16)

            order(RH, lambda j, b: gate_a(j, b, j % 2), last=True)
            for m in range(4, KB):
                for b in range(2):
                    gate_a(m, b, m % 2)
            for p in range(2):
                act.wait_ge(S[f"g_st{p}"], 16 * (KB // 2))

            def gate_r(i, first):
                for p in range(2):
                    m = 2 * i + p
                    for b in range(2):
                        act.wait_ge(d_done[b], USE0["gr"] + 2 * m + 1)
                        if not first:
                            act.wait_ge(d_free[b], USE0["gr"] + 2 * m - 2)
                        apart(act, i)
                        act.activation(sig[:, p, half(b)], ps[:, b, :], ACT.Sigmoid,
                                       bias=smc("b_gate", KB + m)).then_inc(d_free[b], 1)
                    for b in range(2):
                        act.wait_ge(d_free[b], USE0["gr"] + 2 * m + 2)
                    act.dma_start(row(s_mr, m), mxr[:, p, :]).then_inc(S[f"m_st{p}"], 16)
            gate_r(0, True)
            with act.Fori(1, KB // 2) as i:
                gate_r(i, False)

            for p in range(2):
                act.wait_ge(S[f"m_st{p}"], 16 * (KB // 2))
            for j in range(4):
                for b in range(2):
                    act.wait_ge(d_done[b], USE0["lat"] + j + 1)
                    if j < 3:
                        copy(lz[:, j, half(b)], ps[:, b, :]).then_inc(d_free[b], 1)
                    else:
                        copy(zkr[:, half(b)], ps[0:ROPE, b, :]).then_inc(d_free[b], 1)
            for n in range(6):
                act.wait_ge(S["l_sq"], n + 1)
                at_least(act, S["l_ss"], n)
                copy(lsh[:, :], lsq[:, :]).then_inc(S["l_sh"], 1)
            act.wait_ge(S["l_ss"], 6)
            for b in range(2):
                act.activation(lr[:, 0, half(b)], ps[:, 2 + b, :], ACT.Sqrt, scale=1.0 / QR,
                               bias=cnc("eps")).then_inc(S["l_std"], 1)
                act.activation(lr[:, 1, half(b)], ps[:, 4 + b, :], ACT.Sqrt, scale=1.0 / KVR,
                               bias=cnc("eps")).then_inc(S["l_std"], 1)
            for n in range(6):
                b, j = divmod(n, 3)
                act.wait_ge(S["l_c"], n + 1)
                copy(cqh[:, j, half(b)] if j < 2 else ckh[:, half(b)], lz[:, j, half(b)]).then_inc(S["l_hi"], 1)
            R = slice(NOPE, QK)
            for b in range(2):
                act.wait_ge(S["k_T"], b + 1)
                for p in range(2):
                    copy(kbh[R, p, half(b)], ps[R, 6 + b, :]).then_inc(S["k_hi"], 1)

            HW = MH // 2 * QK
            for t in range(NT):
                for b in range(2):
                    act.wait_ge(d_done[b], USE0["qrow"] + t + 1)
                    copy(qrow[:, t, b * HW:(b + 1) * HW], ps[:, b, 0:HW]).then_inc(d_free[b], 1)
            for t in range(NT):
                act.wait_ge(d_done[t % 2], USE0["vrow"] + t // 2 + 1)
                copy(vrh[:, t, :], ps[:, t % 2, :]).then_inc(S["v_evh"], 1)

            def aux_hi(h, n):
                act.wait_ge(S["aux_t"], 4 * h + n + 1)
                b = n % 2
                if n < 2:
                    copy(kbh[0:NOPE, h % 2, half(b)], ps[0:NOPE, 0, :]).then_inc(S["aux_hi"], 1)
                else:
                    copy(mqh[0:QK, h % 2, half(b)], ps[0:QK, 0, :]).then_inc(S["aux_hi"], 1)

            def aux_o_hi(fb, b, bank=0):
                act.wait_ge(S["aux_t"], 4 * MH + 2 * fb + b + 1)
                copy(oth[:, fb, half(b)], ps[:, bank, :]).then_inc(S["aux_hi"], 1)

            def s2(w):
                c = 2 + 2 * (w % 2)
                return ps[:, c:c + 2, :].rearrange("p a n -> p (a n)")

            def m_exp(w):
                n = (w % NT + 1) * P
                act.wait_ge(S["m_neg"], w + 1)
                at_least(act, S["m_ptt"], w - 1)
                at_least(act, S["m_o"], w - 1)
                act.activation(prow[:, w % 2, 0:n], s2(w)[:, 0:n], ACT.Exp, scale=QK ** -0.5,
                               bias=aneg[:, w % 2, 0:1], accum_out=asum[:, w % 2, 0:1]).then_inc(S["m_exp"], 1)

            def m_pth(w):
                n = (w % NT + 1) * P
                act.wait_ge(S["m_ptt"], w + 1)
                at_least(act, S["m_pv"], w - 1)
                copy(pth[:, w % 2, 0:n], ps[:, 6:8, :].rearrange("p a n -> p (a n)")[:, 0:n]).then_inc(S["m_pth"], 1)

            for n in range(4):
                aux_hi(0, n)
            for t in range(XR):
                act.dma_start(xtile[:, t, :], x[t * P:(t + 1) * P, :]).then_inc(S[f"xt_ld{t}"], 16)
            NW = MH * NT
            m_exp(0)
            for w in range(NW):
                h, i = divmod(w, NT)
                m_pth(w)
                if w + 1 < NW:
                    m_exp(w + 1)
                if 1 <= i <= 4 and h + 1 < MH:
                    aux_hi(h + 1, i - 1)
                if h == MH - 1 and 1 <= i <= 6:
                    aux_o_hi((i - 1) // 2, (i - 1) % 2)

            for t in range(NT):
                for b in range(2):
                    act.wait_ge(d_done[b], USE0["xt"] + t + 1)
                    copy(hT[:, CH * b:CH * (b + 1), t * P:(t + 1) * P],
                         ps[:, b, :].rearrange("p (a n) -> p a n", a=CH)).then_inc(d_free[b], 1)
                if t + XR < NT:
                    act.dma_start(xtile[:, t % XR, :], x[(t + XR) * P:(t + XR + 1) * P, :]).then_inc(
                        S[f"xt_ld{t % XR}"], 16)
                if t == 0:
                    for m in range(2):
                        act.dma_start(sab[:, m, :], s_ga[m]).then_inc(S[f"sa_ld{m}"], 16)
                        act.dma_start(mrb[:, m, :], s_mr[m]).then_inc(S[f"mr_ld{m}"], 16)
                if t == 1:
                    for b in range(2):
                        aux_o_hi(3, b, 2 + b)

            for m in range(KB):
                for b in range(2):
                    act.wait_ge(S["mix_m"], 2 * m + b + 1)
                    copy(mih[:, m, half(b)], sab[:, m % 2, half(b)]).then_inc(S["mix_hi"], 1)
                if m + 2 < KB:
                    act.wait_ge(S["mix_lo"], 2 * m + 2)
                    act.dma_start(sab[:, m % 2, :], s_ga[m + 2]).then_inc(S[f"sa_ld{m % 2}"], 16)
                    act.dma_start(mrb[:, m % 2, :], s_mr[m + 2]).then_inc(S[f"mr_ld{m % 2}"], 16)
            act.dma_start(mrow[:, :, :], mem.rearrange("(r p) n -> p r n", p=P)).then_inc(S["mm_ld"], 16)

            def square(n, m, b, u, h_, sq_, gh=None, gname=None):
                act.wait_ge(d_free[b], u + m + 1)
                if not isinstance(m, int) or m > 0 or n > 0:
                    act.wait_ge(S["o_ac"], 2 * KB * n + 2 * m + b - 1)
                apart(act, m)
                act.activation(sq_[:, b, :], blk(h_, m, b * H2, (b + 1) * H2), ACT.Square).then_inc(S["o_sq"], 1)
                if gh is not None and b == 0:
                    copy(blk(gh, m, 0, H2), blk(h_, m, 0, H2), scale=smc(gname, m)).then_inc(S["o_gh"], 1)

            def acc_hi(n, acc_, ach_):
                act.wait_ge(S["o_ac"], 2 * KB * (n + 1))
                copy(ach_[:, :, :], acc_[:, :, :]).then_inc(S["ac_h"], 1)

            def rms(n, out_):
                act.wait_ge(S["ss_t"], n + 1)
                act.activation(out_[:, :, :], ps[:, 2:4, :], ACT.Sqrt, scale=1.0 / D,
                               bias=cnc("eps")).then_inc(S["ss_s"], 1)

            def out_block(m):
                for b in range(2):
                    square(0, m, b, USE0["out"], hT, sq, g0h, "g_cross")
                act.dma_start(row(s_h, m), blk(hT, m)).then_inc(S["h_sp"], 16)
            out_block(0)
            with act.Fori(1, KB) as m:
                out_block(m)
            acc_hi(0, acc, ach)
            act.wait_ge(d_done[1], USE0["out"] + KB)
            for m in range(KB):
                copy(g1h[:, m, :], hT[:, m, H2:T], scale=smc("g_cross", m)).then_inc(S["g1_h"], 1)
            rms(0, rbc)
            act.wait_ge(S["h_sp"], 16 * KB)

            act.wait_ge(S["mm_ld"], 16)
            act.wait_ge(S["rb_r"], 1)
            for r in range(MB):
                at_least(act, S["mm_sq"], r)
                act.activation(sq[:, :, :].rearrange("p a n -> p (a n)"), mrow[:, r, :], ACT.Square,
                               accum_out=mst[:, 0, r:r + 1]).then_inc(S["mm_sq"], 1)
            act.wait_ge(S["mm_sq"], MB)
            act.activation(mst[:, 1, :], mst[:, 0, :], ACT.Sqrt, scale=1.0 / D, bias=cnc("eps")).then_inc(S["mm_st"], 1)
            with act.Fori(0, KB) as m:
                for b in range(2):
                    act.wait_ge(d_free[b], USE0["xq"] + m + 1)
                    apart(act, m)
                    copy(blk(xqh, m, b * H2, (b + 1) * H2), xf[:, b, :]).then_inc(S["xq_h"], 1)
            for k in range(KB):
                act.wait_ge(S["mm_t"], k // 2 + 1)
                c = (k % 2) * NMEM
                copy(mth[:, k, :], ps[:, 4 + k // 2, c:c + NMEM], scale=smc("g_mem", k)).then_inc(S["mm_hi"], 1)
            with act.Fori(0, KB // 2) as i:
                for b in range(2):
                    act.wait_ge(d_done[b], USE0["xkv"] + i + 1)
                    apart(act, i)
                    copy(blk(mkh, 2 * i + b, 0, NMEM), ps[:, b, 0:NMEM]).then_inc(S["kv_h"], 1)

            def v_turned(m):
                act.wait_ge(S["vT_t"], m + 1)
                copy(mvh[:, :, m * P:(m + 1) * P],
                     ps[:, 4, 0:NMEM].rearrange("p (r n) -> p r n", r=MB)).then_inc(S["mv_h"], 1)
            for m in range(KB):
                b = m % 2
                act.wait_ge(d_done[b], USE0["xkv"] + KB // 2 + m // 2 + 1)
                at_least(act, S["vT_t"], m - 1)
                copy(vT[:, b, :], ps[:, b, 0:NMEM]).then_inc(d_free[b], 1)
                if m:
                    v_turned(m - 1)

            def xa_exp(v):
                act.wait_ge(S["xa_n"], v + 1)
                at_least(act, S["xa_t"], v - 1)
                for t in range(CH):
                    bank = 2 + t // 2 if v % 2 == 0 else 4 + t // 2
                    c = (t % 2) * NMEM
                    l = act.activation(pr[:, v % 2, t, :], ps[:, bank, c:c + NMEM], ACT.Exp, scale=XD ** -0.5,
                                       bias=aneg[:, v % 2, t:t + 1], accum_out=asum[:, v % 2, t:t + 1])
                l.then_inc(S["xa_e"], 1)

            def xa_hi(v):
                act.wait_ge(S["xa_t"], v + 1)
                copy(xph[:, v % 2, :], ps[:, 6:8, :].rearrange("p a n -> p (a n)")).then_inc(S["xa_h"], 1)

            def xo_hi(v):
                j, u = divmod(v, 2)
                for b in range(2):
                    act.wait_ge(d_done[b], USE0["xa"] + v + 1)
                    copy(xqh[:, 2 * j + b, half(u)], ps[:, b, :]).then_inc(S["xo_h"], 1)
            xa_exp(0)
            v_turned(KB - 1)
            for m in range(2):
                act.dma_start(hs[:, m, :], s_h[m]).then_inc(S[f"hs_ld{m}"], 16)
            for v in range(2 * XH):
                xa_hi(v)
                if v + 1 < 2 * XH:
                    xa_exp(v + 1)
                if v:
                    xo_hi(v - 1)
            xo_hi(2 * XH - 1)

            for m in range(KB):
                for b in range(2):
                    square(1, m, b, USE0["xo"], hF, sq, f0h, "g_ffn")
                if m + 2 < KB:
                    act.dma_start(hs[:, m % 2, :], s_h[m + 2]).then_inc(S[f"hs_ld{m % 2}"], 16)
            acc_hi(1, acc, ach)
            act.wait_ge(d_done[1], USE0["xo"] + KB)
            for m in range(KB):
                copy(f1h[:, m, :], hF[:, m, H2:T], scale=smc("g_ffn", m)).then_inc(S["g1_h"], 1)
            rms(1, rbF)

            def channels(c, i, u):
                def tap(x_, b):
                    act.wait_ge(d_free[b], u + x_ + 1)
                    if not (isinstance(c, int) and c == 0):
                        act.wait_ge(S["c_lo"] if x_ else S["c_g"], 2 * c + b - 1)
                    y = yb if x_ else ya
                    apart(act, c)
                    act.activation(y[:, half(b)], z[:, 2 + b * H2:2 + (b + 1) * H2], ACT.Identity,
                                   scale=smc("cw2", c + FB * x_), bias=smc("b_conv", c + FB * x_)).then_inc(
                        S["c_y0"], 1)
                tap(0, 0)
                tap(0, 1)
                for b in range(2):
                    act.wait_ge(S["c_y"], 8 * c + 2 * b + 2)
                    act.activation(ya[:, half(b)], ya[:, half(b)], ACT.Silu).then_inc(S["c_s"], 1)
                tap(1, 0)
                tap(1, 1)
                for b in range(2):
                    act.wait_ge(S["c_g"], 2 * c + b + 1)
                    apart(act, i)
                    copy(blk(fah, i, b * H2, (b + 1) * H2), yb[:, half(b)]).then_inc(S["c_hi"], 1)
            c0, u = 0, FF_USE0
            for g, G in enumerate(FGROUPS):
                if g == 0:
                    channels(0, 0, FF_USE0)
                with act.Fori(int(g == 0), G) as i:
                    channels(c0 + i, i, u + 2 * i)
                c0, u = c0 + G, u + 2 * G + KB
            with act.Fori(0, KB) as m:
                for b in range(2):
                    square(2, m, b, FIN_USE0 - KB, hF, sq2)
                    copy(blk(yo, m, b * H2, (b + 1) * H2), blk(hF, m, b * H2, (b + 1) * H2),
                         scale=smc("g_final", m)).then_inc(S["o_y"], 1)
            acc_hi(2, acc2, ach2)
            act.wait_ge(S["ss_t"], 3)
            act.activation(rs8[:, :, :], ps[:, 2, 0:2 * NT].rearrange("p (t c) -> p t c", c=2), ACT.Sqrt, scale=1.0 / D,
                           bias=cnc("eps")).then_inc(S["ss_s"], 1)
            act.wait_ge(S["rb_r"], 3)
            for t in range(NT):
                act.wait_ge(d_done[0], FIN_USE0 + t + 1)
                if t >= 2:
                    act.wait_ge(S[f"out_st{t % 2}"], 16 * (t // 2))
                copy(orows[:, t % 2, 0:H2], ps[:, 0, :], scale=rs8[:, t, 0:1]).then_inc(d_free[0], 1)
                act.wait_ge(d_free[0], FIN_USE0 + t + 1)
                act.wait_ge(d_free[1], FIN_USE0 + t + 1)
                act.dma_start(out[t * P:(t + 1) * P, :], orows[:, t % 2, :]).then_inc(S[f"out_st{t % 2}"], 16)
            for b in range(2):
                act.wait_ge(S[f"out_st{b}"], 16 * (NT // 2))

        @block.vector
        def _(dve):
            def lo(o, full, h_):
                return dve.tensor_tensor(o, full, h_.bitcast(f32), ALU.subtract)

            def stt(o, a, s_, b_, op0, op1):
                return dve.scalar_tensor_tensor(out=o, in0=a, scalar=s_, in1=b_, op0=op0, op1=op1)

            dve.wait_ge(S["par"], 48)
            for o, n in ((ones_r, "ones"), (ident_r, "ident"), (mask_r, "mask")):
                dve.tensor_copy(o[:, :], cn[:, CN0[n]:CN0[n] + P]).then_inc(S["cst"], 1)
            dve.tensor_copy(posf[:, :], posi[:, :]).then_inc(S["cst"], 1)
            for b in range(2):
                c = slice(CH * b, CH * (b + 1))
                dve.wait_ge(S["x_std"], b + 1)
                dve.reciprocal(rst_x[:, c], rst_x[:, c]).then_inc(S["x_rs"], 1)
                dve.wait_ge(S["x_rs"], b + 1)
                for t in range(CH * b, CH * (b + 1)):
                    dve.tensor_scalar(xs[:, t, :], xs[:, t, :], rst_x[:, t:t + 1], None, ALU.mult).then_inc(
                        S["x_row"], 1)
            for n in range(2 * KB):
                b, k = n // KB, n % KB
                dve.wait_ge(S["xT_hi"], n + 1)
                stt(ul[:, k, half(b)], ps[:, 2 + n % 6, :], smc("g_mix", k), uh[:, k, half(b)].bitcast(f32), ALU.mult,
                    ALU.subtract).then_inc(S["xT_lo"], 1)
            step = [0]

            def link(ins):
                step[0] += 1
                ins.then_inc(S["angs"], 1)
                dve.wait_ge(S["angs"], step[0])

            inv = cn[:, CN0["inv"]:CN0["inv"] + NF]
            dve.wait_ge(S["cst"], 4)
            link(dve.tensor_tensor(ang[:, :, :], posf[:, :].unsqueeze(2).to_broadcast([P, NT, NF]),
                                   inv.unsqueeze(1).to_broadcast([P, NT, NF]), ALU.mult))
            link(dve.tensor_scalar(kk[:, :, :], ang[:, :, :], float(1 / (2 * np.pi)), 12582912.0, ALU.mult, ALU.add))
            link(dve.tensor_scalar(kk[:, :, :], kk[:, :, :], -12582912.0, None, ALU.add))
            for part in TWO_PI_PARTS:
                link(stt(ang[:, :, :].rearrange("p a n -> p (a n)"), kk[:, :, :].rearrange("p a n -> p (a n)"), -part,
                         ang[:, :, :].rearrange("p a n -> p (a n)"), ALU.mult, ALU.add))
            link(dve.tensor_scalar(ang[:, :, :], ang[:, :, :], PI, -PI, ALU.min, ALU.max))
            step_abs = stt(kk[:, :, :].rearrange("p a n -> p (a n)"), ang[:, :, :].rearrange("p a n -> p (a n)"), -1.0,
                           ang[:, :, :].rearrange("p a n -> p (a n)"), ALU.mult, ALU.max)
            step_abs.then_inc(S["sinr"], 1)
            dve.wait_ge(S["sinr"], 1)
            dve.tensor_scalar(kk[:, :, :], kk[:, :, :], -1.0, float(np.pi / 2), ALU.mult, ALU.add).then_inc(
                S["angs"], 1)

            def rotate(h, u):
                w = 2 * h + u
                dve.wait_ge(S["rows_qk"], w + 1)
                if isinstance(h, int) and w == 0:
                    dve.wait_ge(S["sins"], 2)
                at_least(dve, S["y_hi"], w - 1)
                at_least(dve, S["s_hi"], w)
                at_least(dve, S["kr_hi"], w)
                co, si = cosT[:, CH * u:CH * (u + 1), 0:R64], sinT[:, CH * u:CH * (u + 1), 0:R64]
                for n, (bank, dst, f, ta, tb) in enumerate(((2, rq, "xi", t1, t2), (3, rk, "zeta", t3, t4))):
                    src = ps[:, bank, :].rearrange("p (a two n) -> p a two n", a=CH, two=2)
                    o = dst[:, :].rearrange("p (a two n) -> p a two n", a=CH, two=2)
                    a_ = ta[:, :].rearrange("p (two a n) -> p two a n", a=CH, two=2)
                    b_ = tb[:, :].rearrange("p (two a n) -> p two a n", a=CH, two=2)
                    g = cnc(f, h)
                    stt(a_[:, 0], src[:, :, 0, :], g, co, ALU.mult, ALU.mult).then_inc(S["rot_t"], 1)
                    stt(b_[:, 0], src[:, :, 1, :], g, si, ALU.mult, ALU.mult).then_inc(S["rot_t"], 1)
                    stt(a_[:, 1], src[:, :, 1, :], g, co, ALU.mult, ALU.mult).then_inc(S["rot_t"], 1)
                    stt(b_[:, 1], src[:, :, 0, :], g, si, ALU.mult, ALU.mult).then_inc(S["rot_t"], 1)
                    dve.wait_ge(S["rot_t"], 8 * w + 4 * n + 4)
                    dve.tensor_tensor(o[:, :, 0, :], a_[:, 0], b_[:, 0], ALU.subtract)
                    l = dve.tensor_tensor(o[:, :, 1, :], a_[:, 1], b_[:, 1], ALU.add)
                l.then_inc(S["rot"], 1)

            def kr_lo(h, u):
                w = 2 * h + u
                dve.wait_ge(S["kr_hi"], w + 1)
                lo(krl[:, :], rk[:, :], krh[:, :]).then_inc(S["kr_lo"], 1)

            def qk_lo(h, u):
                dve.wait_ge(S["qk_hi"], 2 * h + u + 1)
                lo(qtl[:, :], ps[:, 2, :], qth[:, :])
                lo(ktl[:, :], ps[:, 3, :], kth[:, :]).then_inc(S["qk_lo"], 1)

            def v_lo(h, u):
                dve.wait_ge(S["v_hi"], 2 * h + u + 1)
                lo(vl[:, :], ps[:, 4, :], vh[:, :]).then_inc(S["v_lo"], 1)

            def mask_s(h, u):
                w = 2 * h + u
                dve.wait_ge(S["s_t"], w + 1)
                stt(t2[:, :].rearrange("p (a n) -> p a n", a=CH), ps[:, 5, :].rearrange("p (a n) -> p a n", a=CH),
                    cnc("ginv", h), tri.unsqueeze(1).to_broadcast([P, CH, P]), ALU.mult, ALU.mult).then_inc(S["s_m"], 1)

            def s_lo(h, u):
                dve.wait_ge(S["s_hi"], 2 * h + u + 1)
                lo(sl[:, :], t2[:, :], sh[:, :]).then_inc(S["s_lo"], 1)

            def states(h, u):
                w = 2 * h + u
                dve.wait_ge(S["kv_t"], w + 1)
                at_least(dve, S["r_hi"], w)
                if u == 0:
                    dve.memset(rst[:, 0, :], 0.0).then_inc(S["r_st"], 1)
                else:
                    dve.tensor_copy(rst[:, 0, :], rst[:, CH, :]).then_inc(S["r_st"], 1)
                for j in range(CH):
                    dve.wait_ge(S["r_st"], (CH + 1) * w + j + 1)
                    l = stt(rst[:, j + 1, :], rst[:, j, :], cnc("gC", h), ps[:, 4, j * P:(j + 1) * P], ALU.mult,
                            ALU.add).then_inc(S["r_st"], 1)

            def r_lo(h, u):
                dve.wait_ge(S["r_hi"], 2 * h + u + 1)
                lo(rsl[:, :], rst[:, 0:CH, :].rearrange("p a n -> p (a n)"), rsh[:, :]).then_inc(S["r_lo"], 1)

            def norm_y(h, u):
                w = 2 * h + u
                dve.wait_ge(S["y_t"], w + 1)
                at_least(dve, S["std"], w)
                for j in range(CH):
                    dve.bn_stats(bns[:, j, :], ps[:, 6, j * P:(j + 1) * P]).then_inc(S["gn_st"], 1)
                for j in range(CH):
                    dve.wait_ge(S["gn_st"], CH * w + j + 1)
                    apart(dve, h)
                    l = dve.bn_aggr(mvv[:, j, :], bns[:, j, :])
                l.then_inc(S["var"], 1)
                dve.wait_ge(S["std"], w + 1)
                dve.reciprocal(rsd[:, 1, :], rsd[:, 0, :]).then_inc(S["gn_rc"], 1)
                dve.wait_ge(S["gn_rc"], w + 1)
                for j in range(CH):
                    l = dve.tensor_scalar(yn[:, j * P:(j + 1) * P], ps[:, 6, j * P:(j + 1) * P], mvv[:, j, 0:1],
                                          rsd[:, 1, j:j + 1], ALU.subtract, ALU.mult)
                l.then_inc(S["yn_done"], 1)

            def gate_y(h, u):
                w = 2 * h + u
                dve.wait_ge(S["yT_t"], w + 1)
                dve.wait_ge(d_free[u], 4 * h + 4)
                at_least(dve, S["y_hi"], w)
                stt(t1[:, :], ps[:, 7, :], smc("g_ret", h), sg[:, half(u)], ALU.mult, ALU.mult).then_inc(
                    S["yg_done"], 1)
                dve.wait_ge(S["y_hi"], w + 1)
                lo(blk(ytl, h, u * H2, (u + 1) * H2), t1[:, :], blk(yth, h, u * H2, (u + 1) * H2)).then_inc(
                    S["y_lo"], 1)

            def order(h, last=False):
                old = (lambda f, u: None) if isinstance(h, int) and h == 0 else (lambda f, u: f(h - 1, u))
                new = (lambda f, u: None) if last else (lambda f, u: f(h, u))
                old(gate_y, 0)
                old(qk_lo, 1)
                old(v_lo, 1)
                old(mask_s, 1)
                old(s_lo, 1)
                old(states, 1)
                old(r_lo, 1)
                old(norm_y, 1)
                new(rotate, 0)
                new(kr_lo, 0)
                old(gate_y, 1)
                new(qk_lo, 0)
                new(v_lo, 0)
                new(mask_s, 0)
                new(s_lo, 0)
                new(states, 0)
                new(r_lo, 0)
                new(rotate, 1)
                new(kr_lo, 1)
                new(norm_y, 0)

            order(0)
            with dve.Fori(1, RH) as h:
                order(h)
            order(RH, last=True)

            def mul_r(i, first):
                for p in range(2):
                    m = 2 * i + p
                    for b in range(2):
                        dve.wait_ge(d_done[b], USE0["gr"] + 2 * m + 2)
                        dve.wait_ge(d_free[b], USE0["gr"] + 2 * m + 1)
                        if not first:
                            dve.wait_ge(S[f"m_st{p}"], 16 * i)
                        dve.tensor_tensor(mxr[:, p, half(b)], ps[:, b, :], sig[:, p, half(b)],
                                          ALU.mult).then_inc(d_free[b], 1)
            mul_r(0, True)
            with dve.Fori(1, KB // 2) as i:
                mul_r(i, False)

            def sq_lat(n):
                b, j = divmod(n, 3)
                dve.wait_ge(d_free[b], USE0["lat"] + j + 1)
                at_least(dve, S["l_ss"], n)
                dve.tensor_tensor(lsq[:, :], lz[:, j, half(b)], lz[:, j, half(b)], ALU.mult).then_inc(S["l_sq"], 1)
                dve.wait_ge(S["l_sh"], n + 1)
                lo(lsl[:, :], lsq[:, :], lsh[:, :]).then_inc(S["l_sl"], 1)
            dve.wait_ge(S["m_st0"], 16 * (KB // 2))
            dve.wait_ge(S["m_st1"], 16 * (KB // 2))
            dve.memset(krow[:, :, 0:NOPE], 0.0)
            for n in range(6):
                sq_lat(n)
            dve.wait_ge(S["k_row"], 1)
            co, si = cosT[:, :, R64:NF], sinT[:, :, R64:NF]
            src = ps[:, 7, 0:NT * ROPE].rearrange("p (t two n) -> p t two n", t=NT, two=2)
            k1 = kr1[:, :, :].rearrange("p t (two n) -> p t two n", two=2)
            k2 = kr2[:, :, :].rearrange("p t (two n) -> p t two n", two=2)
            for c in range(2):
                dve.tensor_tensor(k1[:, :, c, :], src[:, :, c, :], co, ALU.mult).then_inc(S["k_r1"], 1)
                dve.tensor_tensor(k2[:, :, c, :], src[:, :, 1 - c, :], si, ALU.mult).then_inc(S["k_r1"], 1)
            dve.wait_ge(S["k_r1"], 4)
            dve.tensor_tensor(krow[:, :, NOPE:NOPE + R16], k1[:, :, 0, :], k2[:, :, 0, :], ALU.subtract).then_inc(
                S["k_r2"], 1)
            dve.tensor_tensor(krow[:, :, NOPE + R16:QK], k1[:, :, 1, :], k2[:, :, 1, :], ALU.add).then_inc(
                S["k_r2"], 2)
            for b in range(2):
                dve.wait_ge(S["l_std"], 4)
            dve.reciprocal(lr[:, :, :], lr[:, :, :]).then_inc(S["l_rc"], 1)
            dve.wait_ge(S["l_rc"], 1)
            for n in range(6):
                b, j = divmod(n, 3)
                z_ = lz[:, j, half(b)]
                g = smc("g_q_lat", j) if j < 2 else smc("g_kv_lat")
                stt(z_, z_, g, lr[:, j // 2, half(b)], ALU.mult, ALU.mult).then_inc(S["l_c"], 1)
            for n in range(6):
                b, j = divmod(n, 3)
                dve.wait_ge(S["l_hi"], n + 1)
                h_, l_ = (cqh[:, j, half(b)], cql[:, j, half(b)]) if j < 2 else (ckh[:, half(b)], ckl[:, half(b)])
                lo(l_, lz[:, j, half(b)], h_).then_inc(S["l_lo"], 1)
            R = slice(NOPE, QK)
            for b in range(2):
                dve.wait_ge(S["k_hi"], 2 * b + 2)
                for p in range(2):
                    lo(kbl[R, p, half(b)], ps[R, 6 + b, :], kbh[R, p, half(b)]).then_inc(S["k_lo"], 1)

            for t in range(NT):
                for b in range(2):
                    dve.wait_ge(d_free[b], USE0["qrow"] + t + 1)
                at_least(dve, S["q_rope"], t)
                q = qrow[:, t, :].rearrange("p (h n) -> p h n", h=MH)
                x1, x2 = q[:, :, NOPE:NOPE + R16], q[:, :, NOPE + R16:QK]
                co = cosT[:, t, R64:NF].unsqueeze(1).to_broadcast([P, MH, R16])
                si = sinT[:, t, R64:NF].unsqueeze(1).to_broadcast([P, MH, R16])
                dve.tensor_tensor(qr1[:, :, 0:R16], x1, co, ALU.mult).then_inc(S["q_r1"], 1)
                dve.tensor_tensor(qr1[:, :, R16:ROPE], x2, co, ALU.mult).then_inc(S["q_r1"], 1)
                dve.tensor_tensor(qr2[:, :, 0:R16], x2, si, ALU.mult).then_inc(S["q_r1"], 1)
                dve.tensor_tensor(qr2[:, :, R16:ROPE], x1, si, ALU.mult).then_inc(S["q_r1"], 1)
                dve.wait_ge(S["q_r1"], 4 * t + 4)
                dve.tensor_tensor(x1, qr1[:, :, 0:R16], qr2[:, :, 0:R16], ALU.subtract)
                dve.tensor_tensor(x2, qr1[:, :, R16:ROPE], qr2[:, :, R16:ROPE], ALU.add).then_inc(S["q_rope"], 1)
            for t in range(NT):
                dve.wait_ge(S["v_evh"], t + 1)
                lo(vrl[:, t, :], ps[:, t % 2, :], vrh[:, t, :]).then_inc(d_free[t % 2], 1)

            def aux_lo(h, n):
                dve.wait_ge(S["aux_hi"], 4 * h + n + 1)
                b = n % 2
                r = slice(0, NOPE) if n < 2 else slice(0, QK)
                h_, l_ = (kbh, kbl) if n < 2 else (mqh, mql)
                lo(l_[r, h % 2, half(b)], ps[r, 0, :], h_[r, h % 2, half(b)]).then_inc(S["aux_lo"], 1)

            def aux_o_lo(fb, b, bank=0):
                dve.wait_ge(S["aux_hi"], 4 * MH + 2 * fb + b + 1)
                lo(otl[:, fb, half(b)], ps[:, bank, :], oth[:, fb, half(b)]).then_inc(S["aux_lo"], 1)

            def m_max(w):
                n = (w % NT + 1) * P
                c = 2 + 2 * (w % 2)
                dve.wait_ge(S["m_s"], w + 1)
                at_least(dve, S["m_exp"], w - 1)
                dve.tensor_reduce(amax[:, w % 2, 0:1], ps[:, c:c + 2, :].rearrange("p a n -> p (a n)")[:, 0:n], AX.X,
                                  ALU.max).then_inc(S["m_mx"], 1)
                dve.wait_ge(S["m_mx"], w + 1)
                dve.tensor_scalar(aneg[:, w % 2, 0:1], amax[:, w % 2, 0:1], -QK ** -0.5, None, ALU.mult).then_inc(
                    S["m_neg"], 1)

            def m_ptl(w):
                n = (w % NT + 1) * P
                dve.wait_ge(S["m_pth"], w + 1)
                lo(ptl[:, w % 2, 0:n], ps[:, 6:8, :].rearrange("p a n -> p (a n)")[:, 0:n],
                   pth[:, w % 2, 0:n]).then_inc(S["m_ptl"], 1)

            def m_norm(w):
                h, i = divmod(w, NT)
                dve.wait_ge(S["m_exp"], w + 1)
                dve.reciprocal(ainv[:, w % 2, 0:1], asum[:, w % 2, 0:1]).then_inc(S["m_ri"], 1)
                dve.wait_ge(S["m_ri"], w + 1)
                dve.wait_ge(S["m_pv"], w + 1)
                dve.tensor_scalar(orow[:, i, h * DV:(h + 1) * DV], ps[:, 1, 0:DV], ainv[:, w % 2, 0:1], None,
                                  ALU.mult).then_inc(S["m_o"], 1)
            for n in range(4):
                aux_lo(0, n)
            NW = MH * NT
            m_max(0)
            for w in range(NW):
                h, i = divmod(w, NT)
                if w + 1 < NW:
                    m_max(w + 1)
                m_ptl(w)
                if w:
                    m_norm(w - 1)
                if 1 <= i <= 4 and h + 1 < MH:
                    aux_lo(h + 1, i - 1)
                if h == MH - 1 and 1 <= i <= 6:
                    aux_o_lo((i - 1) // 2, (i - 1) % 2)
            m_norm(NW - 1)
            for b in range(2):
                aux_o_lo(3, b, 2 + b)

            for m in range(KB):
                dve.wait_ge(S[f"sa_ld{m % 2}"], 16 * (m // 2 + 1))
                dve.wait_ge(S[f"mr_ld{m % 2}"], 16 * (m // 2 + 1))
                for b in range(2):
                    a_ = sab[:, m % 2, half(b)]
                    dve.wait_ge(d_done[b], USE0["mix"] + m + 1)
                    dve.tensor_tensor(a_, ps[:, b, :], a_, ALU.mult).then_inc(d_free[b], 1)
                    dve.wait_ge(d_free[b], USE0["mix"] + m + 1)
                    dve.tensor_tensor(a_, a_, mrb[:, m % 2, half(b)], ALU.add).then_inc(S["mix_m"], 1)
                    dve.wait_ge(S["mix_hi"], 2 * m + b + 1)
                    lo(mil[:, m, half(b)], a_, mih[:, m, half(b)]).then_inc(S["mix_lo"], 1)

            def resid(n, m, u, h_, res, acc_, sq_, gh=None, gl=None, gname=None):
                for b in range(2):
                    dve.wait_ge(d_done[b], u)
                    hb = blk(h_, m, b * H2, (b + 1) * H2)
                    dve.tensor_tensor(hb, ps[:, b, :], res(b), ALU.add).then_inc(d_free[b], 1)
                    q = 2 * KB * n + 2 * m + b
                    if gh is not None and b == 0:
                        dve.wait_ge(S["o_gh"], KB * n + m + 1)
                        stt(blk(gl, m, 0, H2), hb, smc(gname, m), blk(gh, m, 0, H2).bitcast(f32), ALU.mult,
                            ALU.subtract).then_inc(S["o_gl"], 1)
                    dve.wait_ge(S["o_sq"], q + 1)
                    at_least(dve, S["o_ac"], q - 1)
                    dve.tensor_tensor(acc_[:, b, :], acc_[:, b, :], sq_[:, b, :], ALU.add).then_inc(S["o_ac"], 1)

            def acc_lo(n, acc_, ach_, acl_):
                dve.wait_ge(S["ac_h"], n + 1)
                lo(acl_[:, :, :], acc_[:, :, :], ach_[:, :, :]).then_inc(S["ac_l"], 1)

            def clear(n, acc_):
                dve.memset(acc_[:, :, :], 0.0).then_inc(S["o_z"], 1)
                dve.wait_ge(S["o_z"], n + 1)

            def g1_lo(n, h_, gh, gl, gname):
                for m in range(KB):
                    dve.wait_ge(S["g1_h"], KB * n + m + 1)
                    stt(gl[:, m, :], h_[:, m, H2:T], smc(gname, m), gh[:, m, :].bitcast(f32), ALU.mult,
                        ALU.subtract).then_inc(S["g1_l"], 1)

            def h0_block(m):
                resid(0, m, USE0["out"] + m + 1, hT, lambda b: blk(hT, m, b * H2, (b + 1) * H2), acc, sq, g0h, g0l,
                      "g_cross")
            clear(0, acc)
            h0_block(0)
            with dve.Fori(1, KB) as m:
                h0_block(m)
            acc_lo(0, acc, ach, acl)
            g1_lo(0, hT, g1h, g1l, "g_cross")
            dve.wait_ge(S["ss_s"], 1)
            dve.reciprocal(rbc[:, :, :], rbc[:, :, :]).then_inc(S["rb_r"], 1)

            dve.wait_ge(S["mm_st"], 1)
            dve.reciprocal(mst[:, 2, :], mst[:, 1, :]).then_inc(S["mm_rc"], 1)
            dve.wait_ge(S["mm_rc"], 1)
            for r in range(MB):
                dve.tensor_scalar(mrow[:, r, :], mrow[:, r, :], mst[:, 2, r:r + 1], None, ALU.mult).then_inc(
                    S["mm_n"], 1)
            dve.wait_ge(S["rb_r"], 1)
            with dve.Fori(0, KB) as m:
                for b in range(2):
                    dve.wait_ge(d_done[b], USE0["xq"] + m + 1)
                    dve.tensor_tensor(xf[:, b, :], ps[:, b, :], rbc[:, b, :], ALU.mult).then_inc(
                        d_free[b], 1)
                    dve.wait_ge(S["xq_h"], 2 * m + b + 1)
                    lo(blk(xql, m, b * H2, (b + 1) * H2), xf[:, b, :], blk(xqh, m, b * H2, (b + 1) * H2)).then_inc(
                        S["xq_l"], 1)
            for k in range(KB):
                dve.wait_ge(S["mm_hi"], 2 * (k // 2) + 2)
                c = (k % 2) * NMEM
                stt(mtl[:, k, :], ps[:, 4 + k // 2, c:c + NMEM], smc("g_mem", k), mth[:, k, :].bitcast(f32), ALU.mult,
                    ALU.subtract).then_inc(S["mm_lo"], 1)
            with dve.Fori(0, KB // 2) as i:
                for b in range(2):
                    dve.wait_ge(S["kv_h"], 2 * i + b + 1)
                    lo(blk(mkl, 2 * i + b, 0, NMEM), ps[:, b, 0:NMEM], blk(mkh, 2 * i + b, 0, NMEM)).then_inc(
                        d_free[b], 1)

            def v_turned(m):
                dve.wait_ge(S["mv_h"], m + 1)
                lo(mvl[:, :, m * P:(m + 1) * P], ps[:, 4, 0:NMEM].rearrange("p (r n) -> p r n", r=MB),
                   mvh[:, :, m * P:(m + 1) * P]).then_inc(S["mv_l"], 1)
            for m in range(KB - 1):
                v_turned(m)

            def xa_max(v):
                c = 2 if v % 2 == 0 else 4
                dve.wait_ge(S["xa_s"], v + 1)
                at_least(dve, S["xa_e"], v - 1)
                if v == 0:
                    dve.wait_ge(S["m_exp"], NW)
                dve.tensor_reduce(amax[:, v % 2, :], ps[:, c:c + 2, :].rearrange("p a (t n) -> p (a t) n", t=2), AX.X,
                                  ALU.max).then_inc(S["xa_m"], 1)
                dve.wait_ge(S["xa_m"], v + 1)
                dve.tensor_scalar(aneg[:, v % 2, :], amax[:, v % 2, :], -XD ** -0.5, None, ALU.mult).then_inc(
                    S["xa_n"], 1)

            def xa_norm(v):
                dve.wait_ge(S["xa_e"], v + 1)
                dve.reciprocal(ainv[:, v % 2, :], asum[:, v % 2, :]).then_inc(S["xa_r"], 1)
                dve.wait_ge(S["xa_r"], v + 1)
                for t in range(CH):
                    l = dve.tensor_scalar(pr[:, v % 2, t, :], pr[:, v % 2, t, :], ainv[:, v % 2, t:t + 1], None,
                                          ALU.mult)
                l.then_inc(S["xa_p"], 1)

            def xa_lo(v):
                dve.wait_ge(S["xa_h"], v + 1)
                lo(xpl[:, v % 2, :], ps[:, 6:8, :].rearrange("p a n -> p (a n)"), xph[:, v % 2, :]).then_inc(
                    S["xa_l"], 1)

            def xo_lo(v):
                j, u = divmod(v, 2)
                for b in range(2):
                    dve.wait_ge(S["xo_h"], 2 * v + b + 1)
                    lo(xql[:, 2 * j + b, half(u)], ps[:, b, :], xqh[:, 2 * j + b, half(u)]).then_inc(
                        d_free[b], 1)
            xa_max(0)
            v_turned(KB - 1)
            xa_norm(0)
            for v in range(2 * XH):
                if v + 1 < 2 * XH:
                    xa_max(v + 1)
                xa_lo(v)
                if v:
                    xo_lo(v - 1)
                if v + 1 < 2 * XH:
                    xa_norm(v + 1)
            xo_lo(2 * XH - 1)

            clear(1, acc)
            for m in range(KB):
                dve.wait_ge(S[f"hs_ld{m % 2}"], 16 * (m // 2 + 1))
                resid(1, m, USE0["xo"] + m + 1, hF, lambda b: hs[:, m % 2, half(b)], acc, sq, f0h, f0l, "g_ffn")
            acc_lo(1, acc, ach, acl)
            g1_lo(1, hF, f1h, f1l, "g_ffn")
            dve.wait_ge(S["ss_s"], 2)
            dve.reciprocal(rbF[:, :, :], rbF[:, :, :]).then_inc(S["rb_r"], 1)
            dve.memset(z[:, 0:2], 0.0).then_inc(S["c_zp"], 1)
            dve.wait_ge(S["c_zp"], 1)
            dve.wait_ge(S["rb_r"], 2)

            def channels(c, i, u):
                def conv(x_, b):
                    q = 4 * c + 2 * x_ + b
                    y = (yb if x_ else ya)[:, half(b)]
                    dve.wait_ge(d_done[b], u + x_ + 1)
                    if x_ or b or not isinstance(c, int):
                        dve.wait_ge(S["c_y"], 2 * q)
                    dve.tensor_tensor(z[:, 2 + b * H2:2 + (b + 1) * H2], ps[:, b, :], rbF[:, b, :],
                                      ALU.mult).then_inc(d_free[b], 1)
                    dve.wait_ge(S["c_y0"], q + 1)
                    stt(y, z[:, 1 + b * H2:1 + (b + 1) * H2], smc("cw1", c + FB * x_), y, ALU.mult, ALU.add).then_inc(
                        S["c_y"], 1)
                    dve.wait_ge(S["c_y"], 2 * q + 1)
                    stt(y, z[:, b * H2:(b + 1) * H2], smc("cw0", c + FB * x_), y, ALU.mult, ALU.add).then_inc(
                        S["c_y"], 1)
                conv(0, 0)
                conv(0, 1)
                conv(1, 0)
                conv(1, 1)
                for b in range(2):
                    y = yb[:, half(b)]
                    dve.wait_ge(S["c_s"], 2 * c + b + 1)
                    dve.wait_ge(S["c_y"], 8 * c + 4 + 2 * b + 2)
                    dve.tensor_tensor(y, y, ya[:, half(b)], ALU.mult).then_inc(S["c_g"], 1)
                for b in range(2):
                    y = yb[:, half(b)]
                    dve.wait_ge(S["c_hi"], 2 * c + b + 1)
                    lo(blk(fal, i, b * H2, (b + 1) * H2), y, blk(fah, i, b * H2, (b + 1) * H2)).then_inc(S["c_lo"], 1)

            c0, u = 0, FF_USE0
            for g, G in enumerate(FGROUPS):
                if g == 0:
                    channels(0, 0, u)
                with dve.Fori(int(g == 0), G) as i:
                    channels(c0 + i, i, u + 2 * i)
                c0, u = c0 + G, u + 2 * G
                if g < len(FGROUPS) - 1:
                    with dve.Fori(0, KB) as m:
                        for b in range(2):
                            hb = blk(hF, m, b * H2, (b + 1) * H2)
                            dve.wait_ge(d_done[b], u + m + 1)
                            dve.tensor_tensor(hb, ps[:, b, :], hb, ALU.add).then_inc(d_free[b], 1)
                else:
                    dve.wait_ge(d_done[0], u + 1)
                    clear(2, acc2)
                    with dve.Fori(0, KB) as m:
                        resid(2, m, u + m + 1, hF, lambda b: blk(hF, m, b * H2, (b + 1) * H2), acc2, sq2)
                u += KB
            acc_lo(2, acc2, ach2, acl2)
            dve.wait_ge(S["ss_s"], 3)
            dve.reciprocal(rs8[:, :, :], rs8[:, :, :]).then_inc(S["rb_r"], 1)
            dve.wait_ge(S["rb_r"], 3)
            for t in range(NT):
                dve.wait_ge(d_done[1], FIN_USE0 + t + 1)
                if t >= 2:
                    dve.wait_ge(S[f"out_st{t % 2}"], 16 * (t // 2))
                dve.tensor_scalar(orows[:, t % 2, H2:D], ps[:, 1, :], rs8[:, t, 0:1], None, ALU.mult).then_inc(
                    d_free[1], 1)


def weight_slabs(w_in, w_uq, w_ukv, w_proj_mla, w_proj_ret, w_out, w_xq, w_xkv, w_xo, w_up, w_down):
    out = np.zeros((NSLAB, P, 1024), np.float32)
    n = 0

    def put(w):
        nonlocal n
        k, m = w.shape
        out[n, :, :k // P * m] = w.reshape(k // P, P, m).transpose(1, 0, 2).reshape(P, -1)
        n += 1

    def cols(w, m, width=P):
        return w[:, m * width:(m + 1) * width]
    for h in range(RH):
        for c in (C_RQ, C_RK, C_RV, C_RG):
            put(w_in[:, c + h * RDK:c + (h + 1) * RDK])
    for m in range(KB):
        put(w_in[:, C_GA + m * P:C_GA + (m + 1) * P])
    for m in range(KB):
        put(w_in[:, C_GR + m * P:C_GR + (m + 1) * P])
        put(cols(w_proj_ret, m))
    for c, e in ((0, P), (P, QR), (C_KV, C_KR), (C_KR, C_RQ)):
        put(w_in[:, c:e])
    put(w_uq[0:P])
    put(w_uq[P:QR])
    kv = w_ukv.reshape(KVR, MH, NOPE + DV)
    put(kv[:, :, :NOPE].reshape(KVR, -1))
    put(kv[:, :, NOPE:].reshape(KVR, -1))
    for m in range(KB // 2):
        put(cols(w_proj_mla, m, 2 * P))
    for w, c in ((w_out, KB), (w_xq, KB), (w_xkv, 2 * KB), (w_xo, KB)):
        for m in range(c):
            put(cols(w, m))
    c0 = 0
    for g in FGROUPS:
        for c in range(c0, c0 + g):
            put(cols(w_up, c))
            put(cols(w_up, FB + c))
        for m in range(KB):
            put(cols(w_down[c0 * P:(c0 + g) * P], m))
        c0 += g
    assert n == NSLAB
    return out


def constants():
    g = 1.0 - np.exp2(-5.0 - np.arange(RH))
    i = np.arange(P)[:, None]
    parts = {
        "ident": np.eye(P), "tri": np.triu(np.ones((P, P))),
        "mask": np.where(np.arange(P)[None, :] > i, -1e30, 0.0), "ones": np.ones((P, P)),
        "inv": np.broadcast_to(np.concatenate([10000.0 ** -(np.arange(n) / n) for n in (R64, R16)]), (P, NF)),
        "xi": g ** (i + 1.0), "zeta": g ** (P - 1.0 - i) * RDK ** -0.5,
        "ginv": np.broadcast_to(g ** -float(P), (P, RH)), "gC": np.broadcast_to(g ** float(P), (P, RH)),
        "eps": np.full((P, 1), EPS)}
    return np.concatenate([parts[k] for k in CN0], axis=1).astype(np.float32)


def kernel(x, mem, positions, g_mix, w_in, b_gate, g_q_lat, w_uq, g_kv_lat, w_ukv, w_proj_mla, g_ret, w_proj_ret,
           w_out, g_cross, g_mem, w_xq, w_xkv, w_xo, g_ffn, w_up, w_conv, b_conv, w_down, g_final):
    import concourse.bacc as bacc
    from concourse.bass_utils import run_bass_kernel_spmd

    a = np.asarray
    w_conv = a(w_conv)[0]
    small = {"g_mix": a(g_mix)[0], "g_cross": a(g_cross)[0], "g_ffn": a(g_ffn)[0], "g_final": a(g_final),
             "g_mem": a(g_mem)[0], "b_gate": a(b_gate)[0], "g_q_lat": a(g_q_lat)[0], "g_kv_lat": a(g_kv_lat)[0],
             "g_ret": a(g_ret)[0], "cw0": w_conv[0], "cw1": w_conv[1], "cw2": w_conv[2], "b_conv": a(b_conv)[0]}
    arrays = {
        "x": np.ascontiguousarray(a(x)[0]), "mem": np.ascontiguousarray(a(mem)[0]),
        "pos": np.ascontiguousarray(a(positions)[0].reshape(NT, P).T),
        "slabs": weight_slabs(*(a(w)[0] for w in (w_in, w_uq, w_ukv, w_proj_mla, w_proj_ret, w_out, w_xq, w_xkv, w_xo,
                                                  w_up, w_down))),
        "small": np.ascontiguousarray(np.concatenate([small[k].reshape(-1, P).T for k, _ in SMALL], axis=1)),
        "const": constants()}
    nc = bacc.Bacc("TRN2", target_bir_lowering=False, num_devices=1)
    args = [nc.dram_tensor(f"in_{k}", v.shape, mybir.dt.from_np(v.dtype), kind="ExternalInput").ap()
            for k, v in arrays.items()]
    out = nc.dram_tensor("out", (T, D), mybir.dt.float32, kind="ExternalOutput").ap()
    build(nc, *args, out)
    r = run_bass_kernel_spmd(nc, [{f"in_{k}": v for k, v in arrays.items()}], core_ids=[0])
    return r.results[0]["out"].reshape(1, T, D)
```

```python
import numpy as np
import concourse.bass as bass
from concourse import mybir
from contextlib import ExitStack

D = 1024
T = 1024
P = 128
H2 = 512
KB = D // P
NT = T // P
CH = H2 // P
NMEM = 256
MB = NMEM // P
RH = 4
RDK = 128
MH = 8
NOPE, ROPE, DV = 64, 32, 64
QK = NOPE + ROPE
QR, KVR = 256, 128
QB = QR // P
XH, XD = 4, 256
FF = 2816
FB = FF // P
FGROUPS = (6, 6, 6, 4)
EPS = 1e-6
QORDER = (1, 3, 2, 0, 5, 7, 6, 4)
AUX_AT = {2: 0, 3: 1, 4: 2, 6: 3}
UNITS = [(h, i) for h in range(MH) for i in QORDER]
PIECE0 = [sum(i // CH + 1 for _, i in UNITS[:w]) for w in range(len(UNITS) + 1)]
BANK0 = [("aux", 0, n) for n in range(4)]
for _w in range(1, len(UNITS) + 1):
    if _w < len(UNITS) and _w % NT in AUX_AT and _w // NT + 1 < MH:
        BANK0.append(("aux", _w // NT + 1, AUX_AT[_w % NT]))
    if _w % CH == 0:
        BANK0.append(("sum", _w // CH - 1))
USE_OF = {e: n for n, e in enumerate(BANK0)}
SLOTS = 4
RAWS = 2
XR = 4
PI = 3.1415925
TWO_PI_PARTS = (6.25, 0.033203125, -1.7821788787841797e-05, -5.2954e-10)

C_KV, C_KR = QR, QR + KVR
C_RQ = C_KR + ROPE
C_RK, C_RV, C_RG = C_RQ + RH * RDK, C_RQ + 2 * RH * RDK, C_RQ + 3 * RH * RDK
C_GA = C_RQ + 4 * RH * RDK
C_GR = C_GA + D


def starts(sizes):
    at, n = {}, 0
    for name, size in sizes:
        at[name] = n
        n += size
    return at, n


SLAB0, FF_SLAB0 = starts((("ret", 4 * RH), ("ga", KB), ("gr", 2 * KB), ("lat", 4), ("mla", 4), ("mix", KB // 2),
                          ("out", KB), ("xq", KB), ("xkv", 2 * KB), ("xo", KB)))
NSLAB = FF_SLAB0 + sum(2 * g + KB for g in FGROUPS)
assert NSLAB % SLOTS == 0 and all(v % SLOTS == 0 for v in SLAB0.values())
USE0, FF_USE0 = starts((("ret", 4 * RH), ("ga", KB), ("gr", 2 * KB), ("lat", 4), ("qrow", NT), ("vrow", NT // 2),
                        ("xt", NT), ("mix", KB), ("out", KB), ("xq", KB), ("xkv", KB), ("xa", 2 * XH), ("xo", KB)))
FIN_USE0 = FF_USE0 + sum(2 * g + KB for g in FGROUPS)
SMALL = (("g_mix", 8), ("g_cross", 8), ("g_ffn", 8), ("g_final", 8), ("g_mem", 8), ("b_gate", 16), ("g_q_lat", 2),
         ("g_kv_lat", 1), ("g_ret", 4), ("cw0", 44), ("cw1", 44), ("cw2", 44), ("b_conv", 44))
SM0, NSMALL = starts(SMALL)
R64, R16 = RDK // 2, ROPE // 2
NF = R64 + R16
CN0, NCONST = starts((("ident", 128), ("tri", 128), ("mask", 128), ("ones", 128), ("inv", NF), ("xi", RH),
                      ("zeta", RH), ("ginv", RH), ("gC", RH), ("eps", 1)))


def build(nc, x, mem, pos, slabs, small, const, out):
    f32, f32r, i32 = mybir.dt.float32, mybir.dt.float32r, mybir.dt.int32
    ALU, ACT, AX = mybir.AluOpType, mybir.ActivationFunctionType, mybir.AxisListType
    ds = bass.ds
    ctx = ExitStack()

    def place(kb, specs):
        with ExitStack() as st:
            if kb:
                st.enter_context(nc.sbuf_tensor(f"below_{specs[0][0]}", [P, int(kb * 256)], f32))
            return [st.enter_context(nc.sbuf_tensor(n, s, f32r if r else f32)) for n, s, r in specs]

    def at_least(eng, s, v):
        if not (isinstance(v, int) and v <= 0):
            eng.wait_ge(s, v)

    def apart(eng, *of):
        if not all(isinstance(v, int) for v in of):
            eng.nop(nofuse=True)

    with ctx:
        def sb(name, shape, dt=f32):
            return ctx.enter_context(nc.sbuf_tensor(name, shape, dt))

        def sem(name):
            return ctx.enter_context(nc.semaphore(name))

        raw = sb("raw", [P, RAWS, 1024])
        wh = sb("wh", [P, SLOTS, 1024], f32r)
        wl = sb("wl", [P, SLOTS, 1024], f32r)
        sm = sb("sm", [P, NSMALL])
        cn = sb("cn", [P, NCONST])
        ones_r = sb("ones_r", [P, P], f32r)
        ident_r = sb("ident_r", [P, P], f32r)
        mask_r = sb("mask_r", [P, P], f32r)
        posi = sb("posi", [P, NT], i32)
        posf = sb("posf", [P, NT])
        ssq = sb("ssq", [P, NT])
        rst_x = sb("rst_x", [P, NT])
        rsm = sb("rsm", [P, NT, 2])
        mst = sb("mst", [P, 3, MB])
        amax, aneg, asum, ainv = (sb(n, [P, 2, CH]) for n in ("amax", "aneg", "asum", "ainv"))
        ps = ctx.enter_context(nc.psum_tensor("ps", [P, 8, H2], f32))

        uh, ul = place(0, [("uh", [P, KB, T], 1), ("ul", [P, KB, T], 1)])
        xs, ang, kk, junk = place(64, [("xs", [P, NT, D], 0), ("ang", [P, NT, NF], 0), ("kk", [P, NT, NF], 0),
                                       ("junk", [P, D], 0)])
        yth, ytl = place(64, [("yth", [P, RH, T], 1), ("ytl", [P, RH, T], 1)])
        cosT, sinT = place(156.5, [("cosT", [P, NT, NF], 0), ("sinT", [P, NT, NF], 0)])
        (zq, zk, zv, sg, t1, t2, rq, rk, qth, qtl, kth, ktl, krh, krl, vh, vl, sh, sl, rst, rsh, rsl, yn, bns, mvv,
         rsd, t3, t4) = place(96, [(n, [P, T], 0) for n in ("zq", "zk", "zv", "sg")]
                      + [(n, [P, H2], 0) for n in ("t1", "t2", "rq", "rk")]
                      + [(n, [P, H2], 1) for n in ("qth", "qtl", "kth", "ktl", "krh", "krl", "vh", "vl", "sh", "sl")]
                      + [("rst", [P, CH + 1, P], 0), ("rsh", [P, H2], 1), ("rsl", [P, H2], 1), ("yn", [P, H2], 0),
                         ("bns", [P, CH, 6], 0), ("mvv", [P, CH, 2], 0), ("rsd", [P, 2, CH], 0), ("t3", [P, H2], 0), ("t4", [P, H2], 0)])
        (sig,) = place(96, [("sig", [P, 2, T], 0)])
        (mxr,) = place(112, [("mxr", [P, 2, T], 0)])
        cqh, cql, ckh, ckl, kbh, kbl, lz, lsq, lr, lrq, zkr, krow, kr1, kr2 = place(64, [
            ("cqh", [P, QB, T], 1), ("cql", [P, QB, T], 1), ("ckh", [P, T], 1), ("ckl", [P, T], 1),
            ("kbh", [P, 2, T], 1), ("kbl", [P, 2, T], 1),
            ("lz", [P, 3, T], 0), ("lsq", [P, T], 0), ("lr", [P, T], 0), ("lrq", [P, NT, 2], 0),
            ("zkr", [ROPE, T], 0), ("krow", [P, NT, QK], 0), ("kr1", [P, NT, ROPE], 0),
            ("kr2", [P, NT, ROPE], 0)])
        vrh, vrl, qrow, qr1, qr2 = place(0, [("vrh", [P, NT, MH * DV], 1), ("vrl", [P, NT, MH * DV], 1),
                                             ("qrow", [P, NT, MH * QK], 0), ("qr1", [P, MH, ROPE], 0),
                                             ("qr2", [P, MH, ROPE], 0)])
        mqh, mql, p0h = place(64, [("mqh", [P, 2, H2], 1), ("mql", [P, 2, H2], 1), ("p0h", [P, CH, H2], 1)])
        (p0l,) = place(56, [("p0l", [P, CH, H2], 1)])
        oT, prow, p1h, p1l = place(104, [("oT", [P, RH, T], 0), ("prow", [P, 2, T], 0),
                                         ("p1h", [P, NT, H2], 1), ("p1l", [P, NT, H2], 1)])
        oth, otl = place(32, [("oth", [P, RH, T], 1), ("otl", [P, RH, T], 1)])
        (xtile,) = place(64, [("xtile", [P, XR, D], 0)])
        (hT,) = place(0, [("hT", [P, KB, T], 0)])
        mih, mil, sab, mrb = place(64, [("mih", [P, KB, T], 1), ("mil", [P, KB, T], 1), ("sab", [P, 2, T], 0),
                                        ("mrb", [P, 2, T], 0)])
        g0h, g0l, g1h, g1l = place(32, [("g0h", [P, KB, H2], 1), ("g0l", [P, KB, H2], 1),
                                        ("g1h", [P, KB, H2], 1), ("g1l", [P, KB, H2], 1)])
        acc, rbc, sq, ach, acl = place(128, [("acc", [P, 2, H2], 0), ("rbc", [P, 2, H2], 0), ("sq", [P, 2, H2], 0),
                                             ("ach", [P, 2, H2], 1), ("acl", [P, 2, H2], 1)])
        (xqh,) = place(0, [("xqh", [P, KB, T], 1)])
        (xql,) = place(96, [("xql", [P, KB, T], 1)])
        xf, mrow = place(148, [("xf", [P, 2, H2], 0), ("mrow", [P, MB, D], 0)])
        mkh, mkl, mvh, mvl = place(32, [("mkh", [P, KB, NMEM], 1), ("mkl", [P, KB, NMEM], 1),
                                        ("mvh", [P, MB, D], 1), ("mvl", [P, MB, D], 1)])
        mth, mtl, vT = place(64, [("mth", [P, KB, NMEM], 1), ("mtl", [P, KB, NMEM], 1),
                                  ("vT", [P, 2, NMEM], 0)])
        pr, xph, xpl = place(64, [("pr", [P, 2, CH, NMEM], 0), ("xph", [P, 2, MB * H2], 1),
                                  ("xpl", [P, 2, MB * H2], 1)])
        (hF,) = place(32, [("hF", [P, KB, T], 0)])
        f0h, f0l = place(64, [("f0h", [P, KB, H2], 1), ("f0l", [P, KB, H2], 1)])
        f1h, f1l = place(0, [("f1h", [P, KB, H2], 1), ("f1l", [P, KB, H2], 1)])
        (hs,) = place(148, [("hs", [P, 2, T], 0)])
        (rbF,) = place(157, [("rbF", [P, 2, H2], 0)])
        fah, fal, z, ya, yb = place(96, [("fah", [P, 6, T], 1), ("fal", [P, 6, T], 1), ("z", [P, T + 2], 0),
                                         ("ya", [P, T], 0), ("yb", [P, T], 0)])
        (yo,) = place(0, [("yo", [P, KB, T], 0)])
        acc2, sq2, ach2, acl2, orows = place(64, [
            ("acc2", [P, 2, H2], 0), ("sq2", [P, 2, H2], 0), ("ach2", [P, 2, H2], 1), ("acl2", [P, 2, H2], 1),
            ("orows", [P, 2, D], 0)])

        ident = cn[:, CN0["ident"]:CN0["ident"] + P]
        tri = cn[:, CN0["tri"]:CN0["tri"] + P]

        def col(t, at, i):
            return t[:, at + i:at + i + 1] if isinstance(i, int) else t[:, ds(at + i, 1)]

        def smc(name, i=0):
            return col(sm, SM0[name], i)

        def cnc(name, i=0):
            return col(cn, CN0[name], i)

        def blk(t, i, lo=0, hi=T):
            return t[:, i, lo:hi] if isinstance(i, int) else t[:, ds(i, 1), lo:hi].rearrange("p a n -> p (a n)")

        def half(b):
            return slice(b * H2, (b + 1) * H2)

        s_ga = nc.dram_tensor("s_ga", (KB, P, T), f32, kind="Internal").ap()
        s_mr = nc.dram_tensor("s_mr", (KB, P, T), f32, kind="Internal").ap()
        s_h = nc.dram_tensor("s_h", (KB, P, T), f32, kind="Internal").ap()

        def row(t, i):
            return t[i] if isinstance(i, int) else t[ds(i, 1)].rearrange("a p n -> (a p) n")

        S = {}
        for name in ("ld0 ld1 w_hi w_kv_hi w_ready w_used par done0 done1 free0 free1 "
                     "x_ld0 x_ld1 x_ld2 x_ld3 x_ld4 x_ld5 x_ld6 x_ld7 x_sq x_std x_rs x_row xT_t xT_hi xT_lo "
                     "cst angs sinr sins "
                     "rows_qk rot_t rot t_qk qk_hi qk_lo kr_hi kr_lo rows_v v_hi v_lo s_t s_m s_hi s_lo kv_t r_st gn_rc "
                     "r_hi r_lo y_t gn_st var std yn_done yT_t yg_done y_hi y_lo "
                     "g_st0 g_st1 m_st0 m_st1 "
                     "l_e l_ss l_std l_rc l_c l_hi l_lo k_row k_r1 k_r2 k_T k_hi k_lo "
                     "q_r1 q_rope v_evh o_hi o_lo aux_t aux_hi aux_lo m_s m_mx m_neg m_exp m_ptt m_pth m_ptl "
                     "m_pv m_ri xt_ld0 xt_ld1 xt_ld2 xt_ld3 sa_ld0 sa_ld1 mr_ld0 mr_ld1 mix_m mix_hi mix_lo "
                     "o_gh o_gl o_sq o_ac o_z ac_h ac_l ss_t ss_s rb_r rb_t rb_c g1_h g1_l h_sp "
                     "xq_h xq_l mm_ld mm_sq mm_st mm_rc mm_n mm_t mm_hi mm_lo kv_h vT_t mv_h mv_l "
                     "xa_s xa_m xa_n xa_e xa_r xa_p xa_t xa_h xa_l xo_h hs_ld0 hs_ld1 "
                     "c_y0 c_y c_s c_g c_hi c_lo c_zp o_y out_st0 out_st1").split():
            S[name] = sem(name)
        d_done, d_free = (S["done0"], S["done1"]), (S["free0"], S["free1"])

        block = ctx.enter_context(nc.Block())

        @block.sync
        def _(sp):
            for t in range(NT):
                sp.dma_start(xs[:, t, :], x[t * P:(t + 1) * P, :]).then_inc(S[f"x_ld{t}"], 16)
                if t == CH - 1:
                    sp.dma_start(cn[:, :], const).then_inc(S["par"], 16)
                    sp.dma_start(sm[:, :], small).then_inc(S["par"], 16)
                    sp.dma_start(posi[:, :], pos).then_inc(S["par"], 16)
                    for j in range(RAWS):
                        sp.dma_start(raw[:, j, :], slabs[j]).then_inc(S[f"ld{j}"], 16)
            for j in range(RAWS, SLOTS):
                sp.wait_ge(S["w_ready"], j - RAWS + 1)
                sp.dma_start(raw[:, j % RAWS, :], slabs[j]).then_inc(S[f"ld{j % RAWS}"], 16)
            with sp.Fori(1, NSLAB // SLOTS) as i:
                for j in range(SLOTS):
                    sp.wait_ge(S["w_ready"], SLOTS * i + (j - RAWS + 1))
                    sp.dma_start(raw[:, j % RAWS, :], row(slabs, SLOTS * i + j)).then_inc(S[f"ld{j % RAWS}"], 16)

        @block.gpsimd
        def _(pool):
            def split(i, j, made=0, both=True):
                s = SLOTS * i + j
                if not both:
                    pool.wait_ge(S["w_kv_hi"], s - SLAB0["xkv"] + 1)
                    pool.tensor_tensor(wl[:, j, :], raw[:, j % RAWS, :], wh[:, j, :].bitcast(f32),
                                       ALU.subtract).then_inc(S["w_ready"], 1)
                    return
                pool.wait_ge(S[f"ld{j % RAWS}"], 16 * (SLOTS // RAWS * i + j // RAWS + 1))
                if not isinstance(i, int) or i > 0:
                    pool.wait_ge(S["w_used"], SLOTS * (i - 1) + j + 1)
                apart(pool, i)
                pool.tensor_scalar(wh[:, j, :], raw[:, j % RAWS, :], 1.0, None, ALU.mult).then_inc(S["w_hi"], 1)
                pool.wait_ge(S["w_hi"], s - made + 1)
                pool.tensor_tensor(wl[:, j, :], raw[:, j % RAWS, :], wh[:, j, :].bitcast(f32),
                                   ALU.subtract).then_inc(S["w_ready"], 1)
            for j in range(SLOTS):
                split(0, j)
            kv, xo = SLAB0["xkv"] // SLOTS, SLAB0["xo"] // SLOTS
            for a, b, made, both in ((1, kv, 0, True), (kv, xo, 0, False), (xo, NSLAB // SLOTS, 2 * KB, True)):
                with pool.Fori(a, b) as i:
                    for j in range(SLOTS):
                        split(i, j, made, both)

        @block.tensor
        def _(pe):
            def mm3(o, lh, ll, rh, rl, start, stop, freed=0, extra=None):
                l = pe.matmul(o, lh, rh, start=start, stop=False)
                if freed:
                    l.then_inc(S["w_used"], freed)
                if extra:
                    extra()
                pe.matmul(o, lh, rl, start=False, stop=False)
                return pe.matmul(o, ll, rh, start=False, stop=stop)

            def wslot(j, k, n=P, at=0, width=None):
                c = k * (width or n) + at
                return wh[:, j, c:c + n], wl[:, j, c:c + n]

            def dense(j, s, u, nk, act, width=P, at=0, m=P, freed=1, first=True, between=(None, None),
                      ready=None):
                if first:
                    pe.wait_ge(S["w_ready"], s + 1)
                for b in range(2):
                    at_least(pe, d_free[b], u)
                    for k in range(nk):
                        if ready:
                            ready(k, b)
                        l = mm3(ps[0:m, b, :], *wslot(j, k, m, at, width), *act(k, b), k == 0, k == nk - 1,
                                freed if first and b == k == 0 else 0)
                    l.then_inc(d_done[b], 1)
                    if between[b]:
                        between[b]()

            def dense_late(j, s, u, nk, act, ready):
                pe.wait_ge(S["w_ready"], s + 1)
                for ks in (range(nk - 1), (nk - 1,)):
                    for b in range(2):
                        for k in ks:
                            if k == 0:
                                pe.wait_ge(d_free[b], u)
                            ready(k, b)
                            l = mm3(ps[:, b, :], *wslot(j, k), *act(k, b), k == 0, k == nk - 1, int(b == k == 0))
                        if nk - 1 in ks:
                            l.then_inc(d_done[b], 1)

            def of(h, l):
                return lambda k, b: (h[:, k, half(b)], l[:, k, half(b)])

            pe.wait_ge(S["par"], 48)
            for n in range(2 * KB):
                b, k = n // KB, n % KB
                if k == 0:
                    pe.wait_ge(S["x_row"], CH * (b + 1))
                if n >= 6:
                    pe.wait_ge(S["xT_lo"], n - 5)
                for j in range(CH):
                    l = pe.transpose(ps[:, 2 + n % 6, j * P:(j + 1) * P], xs[:, CH * b + j, k * P:(k + 1) * P], ident)
                l.then_inc(S["xT_t"], 1)

            def rows_qk(h, u):
                w = 2 * h + u
                pe.wait_ge(d_free[u], 4 * h + 2)
                at_least(pe, S["qk_lo"], w)
                for bank, zz in ((2, zq), (3, zk)):
                    for j in range(CH):
                        c = u * H2 + j * P
                        l = pe.transpose(ps[:, bank, j * P:(j + 1) * P], zz[:, c:c + P], ident)
                l.then_inc(S["rows_qk"], 1)

            def back_qk(h, u):
                pe.wait_ge(S["rot"], 2 * h + u + 1)
                for bank, rr in ((2, rq), (3, rk)):
                    for j in range(CH):
                        l = pe.transpose(ps[:, bank, j * P:(j + 1) * P], rr[:, j * P:(j + 1) * P], ident)
                l.then_inc(S["t_qk"], 1)

            def rows_v(h, u):
                pe.wait_ge(d_free[u], 4 * h + 3)
                at_least(pe, S["r_st"], (CH + 1) * (2 * h + u))
                for j in range(CH):
                    c = u * H2 + j * P
                    l = pe.transpose(ps[:, 4, j * P:(j + 1) * P], zv[:, c:c + P], ident)
                l.then_inc(S["rows_v"], 1)

            def scores(h, u):
                w = 2 * h + u
                pe.wait_ge(S["qk_lo"], w + 1)
                at_least(pe, S["s_m"], w)
                for j in range(CH):
                    c = slice(j * P, (j + 1) * P)
                    l = mm3(ps[:, 5, c], kth[:, c], ktl[:, c], qth[:, c], qtl[:, c], True, True)
                l.then_inc(S["s_t"], 1)

            def states(h, u):
                w = 2 * h + u
                pe.wait_ge(S["kr_lo"], w + 1)
                pe.wait_ge(S["v_lo"], w + 1)
                for j in range(CH):
                    c = slice(j * P, (j + 1) * P)
                    l = mm3(ps[:, 4, c], krh[:, c], krl[:, c], vh[:, c], vl[:, c], True, True)
                l.then_inc(S["kv_t"], 1)

            def outs(h, u):
                w = 2 * h + u
                pe.wait_ge(S["s_lo"], w + 1)
                pe.wait_ge(S["r_lo"], w + 1)
                at_least(pe, S["yn_done"], w)
                for j in range(CH):
                    c = slice(j * P, (j + 1) * P)
                    mm3(ps[:, 6, c], sh[:, c], sl[:, c], vh[:, c], vl[:, c], True, False)
                    l = mm3(ps[:, 6, c], qth[:, c], qtl[:, c], rsh[:, c], rsl[:, c], False, True)
                l.then_inc(S["y_t"], 1)

            def back_y(h, u):
                w = 2 * h + u
                pe.wait_ge(S["yn_done"], w + 1)
                at_least(pe, S["yg_done"], w)
                for j in range(CH):
                    l = pe.transpose(ps[:, 7, j * P:(j + 1) * P], yn[:, j * P:(j + 1) * P], ident)
                l.then_inc(S["yT_t"], 1)

            def between(h, last=False):
                first = isinstance(h, int) and h == 0
                old = (lambda f, u: None) if first else (lambda f, u: f(h - 1, u))
                new = (lambda f, u: None) if last else (lambda f, u: f(h, u))
                return (
                    (lambda: (old(back_y, 0), old(back_qk, 1)), lambda: (old(rows_v, 1), old(scores, 1))),
                    (lambda: old(states, 1), lambda: (old(outs, 1), new(rows_qk, 0))),
                    (lambda: (old(back_y, 1), new(back_qk, 0)), lambda: (new(rows_v, 0), new(scores, 0))),
                    (lambda: (new(states, 0), new(rows_qk, 1)), lambda: new(outs, 0)))

            pe.wait_ge(S["xT_lo"], 2 * KB)
            for j, pair in enumerate(between(0)):
                dense(j, j, j, KB, of(uh, ul), between=pair, freed=int(j > 0))
            with pe.Fori(1, RH) as h:
                for j, pair in enumerate(between(h)):
                    dense(j, 4 * h + j, 4 * h + j, KB, of(uh, ul), between=pair)

            for j, pair in enumerate(between(RH, last=True)):
                dense(j, SLAB0["ga"] + j, USE0["ga"] + j, KB, of(uh, ul), between=pair)
            with pe.Fori(1, KB // 4) as i:
                for j in range(4):
                    dense(j, SLAB0["ga"] + 4 * i + j, USE0["ga"] + 4 * i + j, KB, of(uh, ul))

            pe.wait_ge(S["y_lo"], 2 * RH)
            with pe.Fori(0, KB // 2) as i:
                for j in range(4):
                    s, u = SLAB0["gr"] + 4 * i + j, USE0["gr"] + 4 * i + j
                    if j % 2 == 0:
                        dense(j, s, u, KB, of(uh, ul))
                    else:
                        dense(j, s, u, RH, of(yth, ytl))

            for j in range(4):
                dense(j, SLAB0["lat"] + j, USE0["lat"] + j, KB, of(uh, ul), m=(ROPE if j == 3 else P),
                      width=(ROPE if j == 3 else P))
            ones2 = cn[:, CN0["ones"]:CN0["ones"] + 2]
            pe.wait_ge(d_free[1], USE0["lat"] + 3)
            for t in range(NT):
                for j in range(QB):
                    l = pe.matmul(ps[:, 2, 2 * t:2 * t + 2], lz[:, j, t * P:(t + 1) * P], ones2, start=j == 0,
                                  stop=j == QB - 1)
            l.then_inc(S["l_ss"], 1)
            for b in range(2):
                l = pe.matmul(ps[:, 4 + b, :], cn[:, CN0["ones"]:CN0["ones"] + P], lsq[:, half(b)], start=True,
                              stop=True)
            l.then_inc(S["l_ss"], 1)
            pe.wait_ge(d_free[1], USE0["lat"] + 4)
            for t in range(NT):
                l = pe.transpose(ps[:, 7, t * ROPE:(t + 1) * ROPE], zkr[:, t * P:(t + 1) * P], ident[0:ROPE, 0:ROPE])
            l.then_inc(S["k_row"], 1)

            for j in range(QB):
                pe.wait_ge(S["w_ready"], SLAB0["mla"] + j + 1)
            HW = MH // 2 * QK
            for t in range(NT):
                for b in range(2):
                    pe.wait_ge(d_free[b], USE0["qrow"] + t)
                    for k in range(QB):
                        l = mm3(ps[:, b, 0:HW], cqh[:, k, t * P:(t + 1) * P], cql[:, k, t * P:(t + 1) * P],
                                wh[:, k, b * HW:(b + 1) * HW], wl[:, k, b * HW:(b + 1) * HW], k == 0, k == QB - 1,
                                freed=int(t == b == k == 0))
                    l.then_inc(d_done[b], 1)
            pe.wait_ge(S["k_r2"], 3)
            for b in range(2):
                for j in range(CH):
                    l = pe.transpose(ps[0:QK, 6 + b, j * P:(j + 1) * P], krow[:, CH * b + j, :], ident)
                l.then_inc(S["k_T"], 1)
            pe.wait_ge(S["l_lo"], 2)
            for j in range(2):
                pe.wait_ge(S["w_ready"], SLAB0["mla"] + QB + j + 1)
            for t in range(NT):
                b = t % 2
                pe.wait_ge(d_free[b], USE0["vrow"] + t // 2)
                l = mm3(ps[:, b, :], ckh[:, t * P:(t + 1) * P], ckl[:, t * P:(t + 1) * P], wh[:, 3, 0:MH * DV],
                        wl[:, 3, 0:MH * DV], True, True, freed=(QB if t == 0 else 0))
                l.then_inc(d_done[b], 1)

            def aux(h, n):
                x_ = USE_OF["aux", h, n]
                if x_ == 0:
                    pe.wait_ge(d_free[0], USE0["vrow"] + NT // 2)
                else:
                    pe.wait_ge(S["aux_lo"], x_)
                b = n % 2
                if n < 2:
                    l = mm3(ps[0:NOPE, 0, :], wh[:, 2, h * NOPE:(h + 1) * NOPE], wl[:, 2, h * NOPE:(h + 1) * NOPE],
                            ckh[:, half(b)], ckl[:, half(b)], True, True)
                else:
                    if h == 0 and n == 2:
                        pe.wait_ge(S["q_rope"], NT)
                    for j in range(CH):
                        l = pe.transpose(ps[0:QK, 0, j * P:(j + 1) * P], qrow[:, CH * b + j, h * QK:(h + 1) * QK],
                                         ident)
                        if (h, n, j) == (MH - 1, 2, 0):
                            l.then_inc(S["w_used"], 2)
                l.then_inc(S["aux_t"], 1)

            def m_scores(w):
                h, i = UNITS[w]
                at_least(pe, S["m_exp"], w - 1)
                if w % CH == 0:
                    pe.wait_ge(S["aux_lo"], USE_OF["aux", h, 2 + i // CH] + 1)
                    if w == 0:
                        pe.wait_ge(S["k_lo"], 4)
                p = h % 2
                q = slice(i % CH * P, (i % CH + 1) * P)
                for c in range(i // CH + 1):
                    n = min(CH, i + 1 - c * CH) * P
                    bank = 2 + 2 * (w % 2) + c
                    diag = c == i // CH
                    keys = slice(c * H2, c * H2 + n)

                    def mask(o=ps[:, bank, n - P:n]):
                        pe.matmul(o, ident_r[:, :], mask_r[:, :], start=False, stop=False, skip_group_check=True)
                    l = mm3(ps[:, bank, 0:n], mqh[0:QK, i // CH, q], mql[0:QK, i // CH, q], kbh[0:QK, p, keys],
                            kbl[0:QK, p, keys], True, True, extra=mask if diag else None)
                l.then_inc(S["m_s"], 1)

            def m_turn(w):
                i = UNITS[w][1]
                pe.wait_ge(S["m_exp"], w + 1)
                for n in range(i // CH + 1):
                    q = PIECE0[w] + n
                    at_least(pe, S["m_ptl"], q - 1)
                    for c in range(CH * n, min(CH * (n + 1), i + 1)):
                        l = pe.transpose(ps[:, 6 + q % 2, (c % CH) * P:(c % CH + 1) * P],
                                         prow[:, w % 2, c * P:(c + 1) * P], ident)
                    l.then_inc(S["m_ptt"], 1)

            def m_pv(g):
                h, b = divmod(g, 2)
                pe.wait_ge(S["m_ptl"], PIECE0[CH * (g + 1)])
                if g == 0:
                    for c in range(2):
                        pe.wait_ge(d_free[c], USE0["vrow"] + NT // 2)
                else:
                    pe.wait_ge(S["aux_lo"], USE_OF["sum", g - 1] + 1)
                ph, pl = (p1h, p1l) if b else (p0h, p0l)
                v = slice(h // 2 * P, (h // 2 + 1) * P)

                def one(c, n, start=False, stop=False):
                    qs = slice(max(0, c - CH * b) * P, H2)
                    vv, pp = ((vrh, ph), (vrh, pl), (vrl, ph))[n]
                    return pe.matmul(ps[:, 1, qs], vv[:, c, v], pp[:, c, qs], start=start, stop=stop,
                                     skip_group_check=True)
                one(0, 0, start=True)
                one(0, 1)
                for c in range(1, CH * (b + 1)):
                    for n in range(3):
                        one(c, n)
                one(0, 2, stop=True).then_inc(S["m_pv"], 1)
                pe.wait_ge(S["m_ri"], CH * (g + 1))
                pe.wait_ge(S["aux_lo"], USE_OF["sum", g])
                for j in range(CH):
                    t = UNITS[CH * g + j][1] % CH
                    l = pe.transpose(ps[:, 0, t * P:(t + 1) * P], ainv[:, g % 2, j:j + 1].to_broadcast([P, P]), ident)
                l.then_inc(S["aux_t"], 1)

            for n in range(4):
                aux(0, n)
            NW = len(UNITS)
            m_scores(0)
            m_scores(1)
            for w in range(NW):
                h, r = divmod(w, NT)
                m_turn(w)
                if r in AUX_AT and h + 1 < MH:
                    aux(h + 1, AUX_AT[r])
                if w + 2 < NW:
                    m_scores(w + 2)
                if w and w % CH == 0:
                    m_pv(w // CH - 1)
            m_pv(2 * MH - 1)

            for t in range(NT):
                pe.wait_ge(S[f"xt_ld{t % XR}"], 16 * (t // XR + 1))
                for b in range(2):
                    if t == 0:
                        pe.wait_ge(S["aux_lo"], len(BANK0))
                    else:
                        pe.wait_ge(d_free[b], USE0["xt"] + t)
                    for j in range(CH):
                        k = CH * b + j
                        l = pe.transpose(ps[:, b, j * P:(j + 1) * P], xtile[:, t % XR, k * P:(k + 1) * P], ident)
                    l.then_inc(d_done[b], 1)

            pe.wait_ge(S["o_lo"], 2 * RH)
            for j in range(KB // 2):
                for m in range(2):
                    dense(j, SLAB0["mix"] + j, USE0["mix"] + 2 * j + m, RH, of(oth, otl), width=2 * P, at=m * P,
                          first=(m == 0), freed=int(j > 0))

            dense_late(0, SLAB0["out"], USE0["out"], KB, of(mih, mil),
                       lambda k, b: pe.wait_ge(S["mix_lo"], 2 * k + b + 1))
            for j in range(1, 4):
                dense(j, SLAB0["out"] + j, USE0["out"] + j, KB, of(mih, mil))
            with pe.Fori(1, KB // 4) as i:
                for j in range(4):
                    dense(j, SLAB0["out"] + 4 * i + j, USE0["out"] + 4 * i + j, KB, of(mih, mil))

            def sums(n, ach_, acl_):
                pe.wait_ge(S["ac_l"], n + 1)
                for r in range(NT):
                    b, c, o = r // CH, slice(r % CH * P, (r % CH + 1) * P), ps[:, 2, 2 * r:2 * r + 2]
                    pe.matmul(o, ach_[:, b, c], ones_r[:, 0:2], start=True, stop=False)
                    l = pe.matmul(o, acl_[:, b, c], ones_r[:, 0:2], start=False, stop=True)
                l.then_inc(S["ss_t"], 1)

            def rms_rows(n):
                pe.wait_ge(S["rb_r"], n + 1)
                for r in range(NT):
                    l = pe.transpose(ps[:, 4 + r // CH, r % CH * P:(r % CH + 1) * P],
                                     rsm[:, r, 0:1].to_broadcast([P, P]), ident)
                l.then_inc(S["rb_t"], 1)

            def first_dense(n, s, u, act_):
                def ready(k, b):
                    if b and k == KB - 1:
                        rms_rows(n)
                    pe.wait_ge(S["g1_l"] if b else S["o_gl"], KB * n + k + 1)
                dense(0, s, u, KB, act_, between=(lambda: sums(n, ach, acl), None), ready=ready)

            def halves(h0, l0, h1, l1):
                return lambda k, b: (h0[:, k, :], l0[:, k, :]) if b == 0 else (h1[:, k, :], l1[:, k, :])

            first_dense(0, SLAB0["xq"], USE0["xq"], halves(g0h, g0l, g1h, g1l))
            for j in range(1, 4):
                dense(j, SLAB0["xq"] + j, USE0["xq"] + j, KB, halves(g0h, g0l, g1h, g1l))
            with pe.Fori(1, KB // 4) as i:
                for j in range(4):
                    dense(j, SLAB0["xq"] + 4 * i + j, USE0["xq"] + 4 * i + j, KB, halves(g0h, g0l, g1h, g1l))

            pe.wait_ge(S["mm_n"], MB)
            for n in range(KB // 2):
                for k in range(2):
                    for r in range(MB):
                        l = pe.transpose(ps[:, 4 + n, (2 * k + r) * P:(2 * k + r + 1) * P],
                                         mrow[:, r, (2 * n + k) * P:(2 * n + k + 1) * P], ident)
                l.then_inc(S["mm_t"], 1)
            pe.wait_ge(S["mm_lo"], KB)

            def mem_out(i, j, base):
                s = SLAB0["xkv"] + base + 4 * i + j
                b = j % 2
                pe.wait_ge(S["w_ready"], s + 1)
                pe.wait_ge(d_free[b], USE0["xkv"] + base // 2 + 2 * i + j // 2)
                for k in range(KB):
                    l = mm3(ps[:, b, 0:NMEM], *wslot(j, k), mth[:, k, :], mtl[:, k, :], k == 0, k == KB - 1,
                            freed=int(k == 0))
                l.then_inc(d_done[b], 1)

            with pe.Fori(0, 2) as i:
                for j in range(4):
                    mem_out(i, j, 0)

            def value_rows(m, b):
                pe.wait_ge(d_free[b], USE0["xkv"] + (KB + m) // 2 + 1)
                at_least(pe, S["mv_l"], m)
                for r in range(MB):
                    l = pe.transpose(ps[:, 4, r * P:(r + 1) * P], vT[:, b, r * P:(r + 1) * P], ident)
                l.then_inc(S["vT_t"], 1)
            for i in range(2):
                for j in range(4):
                    mem_out(i, j, KB)
                    m = 4 * i + j
                    if m:
                        value_rows(m - 1, (m - 1) % 2)
            def xa_s(v):
                j, b = divmod(v, 2)
                at_least(pe, S["xa_e"], v - 1)
                for t in range(CH):
                    bank = 2 + t // 2 if v % 2 == 0 else 4 + t // 2
                    c = (t % 2) * NMEM
                    q = slice(b * H2 + t * P, b * H2 + (t + 1) * P)
                    for k in range(2):
                        l = mm3(ps[:, bank, c:c + NMEM], xqh[:, 2 * j + k, q], xql[:, 2 * j + k, q],
                                mkh[:, 2 * j + k, :], mkl[:, 2 * j + k, :], k == 0, k == 1)
                l.then_inc(S["xa_s"], 1)

            def xa_t(v):
                pe.wait_ge(S["xa_p"], v + 1)
                at_least(pe, S["xa_l"], v)
                for k in range(MB):
                    for t in range(CH):
                        l = pe.transpose(ps[:, 6 + k, t * P:(t + 1) * P], pr[:, v % 2, t, k * P:(k + 1) * P], ident)
                l.then_inc(S["xa_t"], 1)

            def xa_pv(v):
                j = v // 2
                pe.wait_ge(S["xa_l"], v + 1)
                if v == 0:
                    pe.wait_ge(S["mv_l"], KB)
                for b in range(2):
                    pe.wait_ge(d_free[b], USE0["xa"] + v)
                    for k in range(MB):
                        c = slice(j * XD + b * P, j * XD + (b + 1) * P)
                        l = mm3(ps[:, b, :], mvh[:, k, c], mvl[:, k, c], xph[:, v % 2, k * H2:(k + 1) * H2],
                                xpl[:, v % 2, k * H2:(k + 1) * H2], k == 0, k == MB - 1)
                    l.then_inc(d_done[b], 1)

            pe.wait_ge(S["xq_l"], 2 * KB)
            for b in range(2):
                pe.wait_ge(d_free[b], USE0["xkv"] + KB)
            xa_s(0)
            value_rows(KB - 1, (KB - 1) % 2)
            pe.wait_ge(S["mv_l"], KB)
            for v in range(2 * XH):
                if v + 1 < 2 * XH:
                    xa_s(v + 1)
                xa_t(v)
                if v:
                    xa_pv(v - 1)
            xa_pv(2 * XH - 1)

            for b in range(2):
                pe.wait_ge(d_free[b], USE0["xo"])
            with pe.Fori(0, KB // 4) as i:
                for j in range(4):
                    dense(j, SLAB0["xo"] + 4 * i + j, USE0["xo"] + 4 * i + j, KB, of(xqh, xql))

            s, u, blocks = FF_SLAB0, FF_USE0, 0
            for g, G in enumerate(FGROUPS):
                n0 = 0
                if g == 0:
                    first_dense(1, s, u, halves(f0h, f0l, f1h, f1l))
                    for j in range(1, 4):
                        dense(j, s + j, u + j, KB, halves(f0h, f0l, f1h, f1l))
                    n0 = 1
                with pe.Fori(n0, G // 2) as i:
                    for j in range(4):
                        dense(j, s + 4 * i + j, u + 4 * i + j, KB, halves(f0h, f0l, f1h, f1l))
                s, u, blocks = s + 2 * G, u + 2 * G, blocks + G
                dense_late(0, s, u, G, of(fah, fal),
                           lambda k, b: pe.wait_ge(S["c_lo"], 2 * (blocks - G + k) + b + 1))
                for j in range(1, 4):
                    dense(j, s + j, u + j, G, of(fah, fal))
                with pe.Fori(1, KB // 4) as i:
                    for j in range(4):
                        dense(j, s + 4 * i + j, u + 4 * i + j, G, of(fah, fal))
                s, u = s + KB, u + KB
            pe.wait_ge(S["o_y"], 2 * KB)
            for t in range(NT):
                for b in range(2):
                    pe.wait_ge(d_free[b], FIN_USE0 + t)
                    for j in range(CH):
                        l = pe.transpose(ps[:, b, j * P:(j + 1) * P], yo[:, CH * b + j, t * P:(t + 1) * P], ident)
                    l.then_inc(d_done[b], 1)
                if t == 0:
                    sums(2, ach2, acl2)

        @block.scalar
        def _(act):
            def copy(o, i, **kw):
                return act.activation(o, i, ACT.Copy, **kw)

            for t in range(NT):
                act.wait_ge(S[f"x_ld{t}"], 16)
                at_least(act, S["x_sq"], t)
                act.activation(junk[:, :], xs[:, t, :], ACT.Square, accum_out=ssq[:, t:t + 1]).then_inc(S["x_sq"], 1)
                if t % CH == CH - 1:
                    b = t // CH
                    act.wait_ge(S["x_sq"], t + 1)
                    if b == 0:
                        act.wait_ge(S["par"], 48)
                    act.activation(rst_x[:, CH * b:CH * (b + 1)], ssq[:, CH * b:CH * (b + 1)], ACT.Sqrt,
                                   scale=1.0 / D, bias=cnc("eps")).then_inc(S["x_std"], 1)
            for n in range(2 * KB):
                b, k = n // KB, n % KB
                act.wait_ge(S["xT_t"], n + 1)
                copy(uh[:, k, half(b)], ps[:, 2 + n % 6, :], scale=smc("g_mix", k)).then_inc(S["xT_hi"], 1)
            act.wait_ge(S["angs"], 9)
            act.activation(sinT[:, :, :], ang[:, :, :], ACT.Sin).then_inc(S["sins"], 1)
            act.activation(cosT[:, :, :], kk[:, :, :], ACT.Sin).then_inc(S["sins"], 1)
            act.wait_ge(S["sins"], 2)

            def evac(h, j, b):
                act.wait_ge(d_done[b], 4 * h + j + 1)
                if j == 3:
                    at_least(act, S["yg_done"], 2 * h + b - 1)
                    act.activation(sg[:, half(b)], ps[:, b, :], ACT.Silu).then_inc(d_free[b], 1)
                else:
                    copy((zq, zk, zv)[j][:, half(b)], ps[:, b, :]).then_inc(d_free[b], 1)

            def kr_hi(h, u):
                act.wait_ge(S["rot"], 2 * h + u + 1)
                copy(krh[:, :], rk[:, :]).then_inc(S["kr_hi"], 1)

            def qk_hi(h, u):
                act.wait_ge(S["t_qk"], 2 * h + u + 1)
                copy(qth[:, :], ps[:, 2, :])
                copy(kth[:, :], ps[:, 3, :]).then_inc(S["qk_hi"], 1)

            def v_hi(h, u):
                act.wait_ge(S["rows_v"], 2 * h + u + 1)
                copy(vh[:, :], ps[:, 4, :]).then_inc(S["v_hi"], 1)

            def s_hi(h, u):
                act.wait_ge(S["s_m"], 2 * h + u + 1)
                copy(sh[:, :], t2[:, :]).then_inc(S["s_hi"], 1)

            def r_hi(h, u):
                act.wait_ge(S["r_st"], (CH + 1) * (2 * h + u + 1))
                copy(rsh[:, :], rst[:, 0:CH, :].rearrange("p a n -> p (a n)")).then_inc(S["r_hi"], 1)

            def y_std(h, u):
                act.wait_ge(S["var"], 2 * h + u + 1)
                act.activation(rsd[:, 0, :], mvv[:, :, 1], ACT.Sqrt, bias=cnc("eps")).then_inc(S["std"], 1)

            def y_hi(h, u):
                act.wait_ge(S["yg_done"], 2 * h + u + 1)
                apart(act, h)
                copy(blk(yth, h, u * H2, (u + 1) * H2), t1[:, :]).then_inc(S["y_hi"], 1)

            def order(h, ev, last=False):
                old = (lambda f, u: None) if isinstance(h, int) and h == 0 else (lambda f, u: f(h - 1, u))
                new = (lambda f, u: None) if last else (lambda f, u: f(h, u))
                ev(0, 0)
                old(y_hi, 0)
                old(qk_hi, 1)
                ev(0, 1)
                old(v_hi, 1)
                old(s_hi, 1)
                ev(1, 0)
                old(r_hi, 1)
                ev(1, 1)
                old(y_std, 1)
                new(kr_hi, 0)
                ev(2, 0)
                old(y_hi, 1)
                new(qk_hi, 0)
                ev(2, 1)
                new(v_hi, 0)
                new(s_hi, 0)
                ev(3, 0)
                new(r_hi, 0)
                new(kr_hi, 1)
                ev(3, 1)
                new(y_std, 0)

            order(0, lambda j, b: evac(0, j, b))
            with act.Fori(1, RH) as h:
                order(h, lambda j, b: evac(h, j, b))

            def gate_a(m, b, p):
                act.wait_ge(d_done[b], USE0["ga"] + m + 1)
                if b == 0 and m >= 2:
                    act.wait_ge(S[f"g_st{p}"], 16 * (m // 2))
                act.activation(sig[:, p, half(b)], ps[:, b, :], ACT.Sigmoid,
                               bias=smc("b_gate", m)).then_inc(d_free[b], 1)
                if b == 1:
                    for c in range(2):
                        act.wait_ge(d_free[c], USE0["ga"] + m + 1)
                    act.dma_start(row(s_ga, m), sig[:, p, :]).then_inc(S[f"g_st{p}"], 16)

            order(RH, lambda j, b: gate_a(j, b, j % 2), last=True)
            for m in range(4, KB):
                for b in range(2):
                    gate_a(m, b, m % 2)
            for p in range(2):
                act.wait_ge(S[f"g_st{p}"], 16 * (KB // 2))

            def gate_r(i, first):
                for p in range(2):
                    m = 2 * i + p
                    for b in range(2):
                        act.wait_ge(d_done[b], USE0["gr"] + 2 * m + 1)
                        if not first:
                            act.wait_ge(d_free[b], USE0["gr"] + 2 * m - 2)
                        apart(act, i)
                        act.activation(sig[:, p, half(b)], ps[:, b, :], ACT.Sigmoid,
                                       bias=smc("b_gate", KB + m)).then_inc(d_free[b], 1)
                    for b in range(2):
                        act.wait_ge(d_free[b], USE0["gr"] + 2 * m + 2)
                    act.dma_start(row(s_mr, m), mxr[:, p, :]).then_inc(S[f"m_st{p}"], 16)
            gate_r(0, True)
            with act.Fori(1, KB // 2) as i:
                gate_r(i, False)

            for p in range(2):
                act.wait_ge(S[f"m_st{p}"], 16 * (KB // 2))
            for j in range(4):
                for b in range(2):
                    act.wait_ge(d_done[b], USE0["lat"] + j + 1)
                    if j < QB:
                        copy(cqh[:, j, half(b)], ps[:, b, :], scale=smc("g_q_lat", j))
                        act.activation(lz[:, j, half(b)], ps[:, b, :], ACT.Square).then_inc(S["l_e"], 1)
                    elif j == QB:
                        copy(lz[:, j, half(b)], ps[:, b, :])
                        act.activation(lsq[:, half(b)], ps[:, b, :], ACT.Square).then_inc(d_free[b], 1)
                    else:
                        copy(zkr[:, half(b)], ps[0:ROPE, b, :]).then_inc(d_free[b], 1)
            act.wait_ge(S["l_ss"], 1)
            act.activation(lrq[:, :, :], ps[:, 2, 0:2 * NT].rearrange("p (t c) -> p t c", c=2), ACT.Sqrt,
                           scale=1.0 / QR, bias=cnc("eps")).then_inc(S["l_std"], 1)
            act.wait_ge(S["l_ss"], 2)
            act.activation(lr[:, :], ps[:, 4:6, :].rearrange("p a n -> p (a n)"), ACT.Sqrt, scale=1.0 / KVR,
                           bias=cnc("eps")).then_inc(S["l_std"], 1)
            act.wait_ge(S["l_rc"], 1)

            HW = MH // 2 * QK
            for t in range(NT):
                for b in range(2):
                    act.wait_ge(d_done[b], USE0["qrow"] + t + 1)
                    copy(qrow[:, t, b * HW:(b + 1) * HW], ps[:, b, 0:HW], scale=lrq[:, t, 0:1]).then_inc(
                        d_free[b], 1)
                if t == 1:
                    for b in range(2):
                        act.wait_ge(S["l_c"], b + 1)
                        copy(ckh[:, half(b)], lz[:, QB, half(b)]).then_inc(S["l_hi"], 1)
            R = slice(NOPE, QK)
            for b in range(2):
                act.wait_ge(S["k_T"], b + 1)
                for p in range(2):
                    copy(kbh[R, p, half(b)], ps[R, 6 + b, :]).then_inc(S["k_hi"], 1)

            for t in range(NT):
                act.wait_ge(d_done[t % 2], USE0["vrow"] + t // 2 + 1)
                copy(vrh[:, t, :], ps[:, t % 2, :]).then_inc(S["v_evh"], 1)

            def aux_hi(h, n):
                act.wait_ge(S["aux_t"], USE_OF["aux", h, n] + 1)
                b = n % 2
                if n < 2:
                    copy(kbh[0:NOPE, h % 2, half(b)], ps[0:NOPE, 0, :]).then_inc(S["aux_hi"], 1)
                else:
                    copy(mqh[0:QK, b, :], ps[0:QK, 0, :]).then_inc(S["aux_hi"], 1)

            def m_sum(g):
                h, b = divmod(g, 2)
                r = slice(h % 2 * DV, (h % 2 + 1) * DV)
                act.wait_ge(S["aux_t"], USE_OF["sum", g] + 1)
                copy(oT[r, h // 2, half(b)], ps[r, 0, :]).then_inc(S["aux_hi"], 1)

            def o_hi(fb, b):
                act.wait_ge(S["aux_lo"], USE_OF["sum", 4 * fb + 2 + b] + 1)
                copy(oth[:, fb, half(b)], oT[:, fb, half(b)]).then_inc(S["o_hi"], 1)

            def s2(w):
                c = 2 + 2 * (w % 2)
                return ps[:, c:c + 2, :].rearrange("p a n -> p (a n)")

            def m_exp(w):
                n = (UNITS[w][1] + 1) * P
                act.wait_ge(S["m_neg"], w + 1)
                if w >= 2:
                    act.wait_ge(S["m_ptt"], PIECE0[w - 1])
                act.activation(prow[:, w % 2, 0:n], s2(w)[:, 0:n], ACT.Exp, scale=QK ** -0.5,
                               bias=aneg[:, 0, w % 4:w % 4 + 1], accum_out=asum[:, 0, w % 4:w % 4 + 1]).then_inc(S["m_exp"], 1)

            def m_pth(w):
                i, g = UNITS[w][1], w // CH
                at_least(act, S["m_pv"], g - 1)
                for n in range(i // CH + 1):
                    q = PIECE0[w] + n
                    c0, c1 = CH * n, min(CH * (n + 1), i + 1)
                    act.wait_ge(S["m_ptt"], q + 1)
                    copy((p1h if g % 2 else p0h)[:, c0:c1, i % CH * P:(i % CH + 1) * P],
                         ps[:, 6 + q % 2, 0:(c1 - c0) * P].rearrange("p (a n) -> p a n", n=P)).then_inc(
                        S["m_pth"], 1)

            for n in range(4):
                aux_hi(0, n)
            NW = len(UNITS)
            m_exp(0)
            for w in range(NW):
                h, r = divmod(w, NT)
                if w > CH and w % CH == 1:
                    m_sum(w // CH - 1)
                m_pth(w)
                if w + 1 < NW:
                    m_exp(w + 1)
                if r in AUX_AT and h + 1 < MH:
                    aux_hi(h + 1, AUX_AT[r])
                if h == MH - 1 and r < 4:
                    o_hi(r // 2, r % 2)
                if h == MH - 1 and r >= 6:
                    o_hi(2, r - 6)
            for t in range(XR):
                act.dma_start(xtile[:, t, :], x[t * P:(t + 1) * P, :]).then_inc(S[f"xt_ld{t}"], 16)
            m_sum(2 * MH - 1)
            for b in range(2):
                o_hi(3, b)

            for t in range(NT):
                for b in range(2):
                    act.wait_ge(d_done[b], USE0["xt"] + t + 1)
                    copy(hT[:, CH * b:CH * (b + 1), t * P:(t + 1) * P],
                         ps[:, b, :].rearrange("p (a n) -> p a n", a=CH)).then_inc(d_free[b], 1)
                if t + XR < NT:
                    act.dma_start(xtile[:, t % XR, :], x[(t + XR) * P:(t + XR + 1) * P, :]).then_inc(
                        S[f"xt_ld{t % XR}"], 16)
                if t == 0:
                    for m in range(2):
                        act.dma_start(sab[:, m, :], s_ga[m]).then_inc(S[f"sa_ld{m}"], 16)
                        act.dma_start(mrb[:, m, :], s_mr[m]).then_inc(S[f"mr_ld{m}"], 16)

            for m in range(KB):
                for b in range(2):
                    act.wait_ge(S["mix_m"], 2 * m + b + 1)
                    copy(mih[:, m, half(b)], sab[:, m % 2, half(b)]).then_inc(S["mix_hi"], 1)
                if m + 2 < KB:
                    act.wait_ge(S["mix_lo"], 2 * m + 2)
                    act.dma_start(sab[:, m % 2, :], s_ga[m + 2]).then_inc(S[f"sa_ld{m % 2}"], 16)
                    act.dma_start(mrb[:, m % 2, :], s_mr[m + 2]).then_inc(S[f"mr_ld{m % 2}"], 16)
            act.dma_start(mrow[:, :, :], mem.rearrange("(r p) n -> p r n", p=P)).then_inc(S["mm_ld"], 16)

            def square(n, m, b, u, h_, sq_, gh=None, gname=None):
                act.wait_ge(d_free[b], u + m + 1)
                if not isinstance(m, int) or m > 0 or n > 0:
                    act.wait_ge(S["o_ac"], 2 * KB * n + 2 * m + b - 1)
                apart(act, m)
                act.activation(sq_[:, b, :], blk(h_, m, b * H2, (b + 1) * H2), ACT.Square).then_inc(S["o_sq"], 1)
                if gh is not None and b == 0:
                    copy(blk(gh, m, 0, H2), blk(h_, m, 0, H2), scale=smc(gname, m)).then_inc(S["o_gh"], 1)

            def acc_hi(n, acc_, ach_):
                act.wait_ge(S["o_ac"], 2 * KB * (n + 1))
                copy(ach_[:, :, :], acc_[:, :, :]).then_inc(S["ac_h"], 1)

            def rms(n):
                act.wait_ge(S["ss_t"], n + 1)
                act.activation(rsm[:, :, :], ps[:, 2, 0:2 * NT].rearrange("p (t c) -> p t c", c=2), ACT.Sqrt,
                               scale=1.0 / D, bias=cnc("eps")).then_inc(S["ss_s"], 1)

            def rms_copy(n, out_):
                act.wait_ge(S["rb_t"], n + 1)
                copy(out_[:, :, :], ps[:, 4:6, :]).then_inc(S["rb_c"], 1)

            def out_block(m):
                for b in range(2):
                    square(0, m, b, USE0["out"], hT, sq, g0h, "g_cross")
                act.dma_start(row(s_h, m), blk(hT, m)).then_inc(S["h_sp"], 16)
            out_block(0)
            with act.Fori(1, KB) as m:
                out_block(m)
            acc_hi(0, acc, ach)
            act.wait_ge(d_done[1], USE0["out"] + KB)
            for m in range(KB):
                copy(g1h[:, m, :], hT[:, m, H2:T], scale=smc("g_cross", m)).then_inc(S["g1_h"], 1)
            rms(0)
            rms_copy(0, rbc)
            act.wait_ge(S["h_sp"], 16 * KB)

            def slab_hi(n, j):
                s = SLAB0["xkv"] + n + j
                act.wait_ge(S[f"ld{j % RAWS}"], 16 // RAWS * (s - j % RAWS) + 16)
                act.wait_ge(S["w_used"], s - SLOTS + 1)
                copy(wh[:, j % SLOTS, :], raw[:, j % RAWS, :]).then_inc(S["w_kv_hi"], 1)

            def xq_block(m):
                for b in range(2):
                    act.wait_ge(d_free[b], USE0["xq"] + m + 1)
                    apart(act, m)
                    copy(blk(xqh, m, b * H2, (b + 1) * H2), xf[:, b, :]).then_inc(S["xq_h"], 1)
            with act.Fori(0, KB - SLOTS) as m:
                xq_block(m)
            act.wait_ge(S["mm_ld"], 16)
            for r in range(MB):
                at_least(act, S["mm_sq"], r)
                act.activation(sq[:, :, :].rearrange("p a n -> p (a n)"), mrow[:, r, :], ACT.Square,
                               accum_out=mst[:, 0, r:r + 1]).then_inc(S["mm_sq"], 1)
            act.wait_ge(S["mm_sq"], MB)
            act.activation(mst[:, 1, :], mst[:, 0, :], ACT.Sqrt, scale=1.0 / D, bias=cnc("eps")).then_inc(S["mm_st"], 1)
            for j in range(SLOTS):
                xq_block(KB - SLOTS + j)
                if j < SLOTS - 1:
                    slab_hi(0, j)
            for k in range(KB):
                act.wait_ge(S["mm_t"], k // 2 + 1)
                c = (k % 2) * NMEM
                copy(mth[:, k, :], ps[:, 4 + k // 2, c:c + NMEM], scale=smc("g_mem", k)).then_inc(S["mm_hi"], 1)
            slab_hi(0, SLOTS - 1)
            with act.Fori(0, KB // SLOTS) as i:
                for j in range(SLOTS):
                    b = j % 2
                    act.wait_ge(d_done[b], USE0["xkv"] + 2 * i + j // 2 + 1)
                    apart(act, i)
                    copy(blk(mkh, SLOTS * i + j, 0, NMEM), ps[:, b, 0:NMEM]).then_inc(S["kv_h"], 1)
                    slab_hi(SLOTS * (i + 1), j)

            def v_turned(m):
                act.wait_ge(S["vT_t"], m + 1)
                copy(mvh[:, :, m * P:(m + 1) * P],
                     ps[:, 4, 0:NMEM].rearrange("p (r n) -> p r n", r=MB)).then_inc(S["mv_h"], 1)
            for m in range(KB):
                b = m % 2
                act.wait_ge(d_done[b], USE0["xkv"] + KB // 2 + m // 2 + 1)
                at_least(act, S["vT_t"], m - 1)
                copy(vT[:, b, :], ps[:, b, 0:NMEM]).then_inc(d_free[b], 1)
                if m < SLOTS:
                    slab_hi(KB + SLOTS, m)
                if m:
                    v_turned(m - 1)

            def xa_exp(v):
                act.wait_ge(S["xa_n"], v + 1)
                at_least(act, S["xa_t"], v - 1)
                for t in range(CH):
                    bank = 2 + t // 2 if v % 2 == 0 else 4 + t // 2
                    c = (t % 2) * NMEM
                    l = act.activation(pr[:, v % 2, t, :], ps[:, bank, c:c + NMEM], ACT.Exp, scale=XD ** -0.5,
                                       bias=aneg[:, v % 2, t:t + 1], accum_out=asum[:, v % 2, t:t + 1])
                l.then_inc(S["xa_e"], 1)

            def xa_hi(v):
                act.wait_ge(S["xa_t"], v + 1)
                copy(xph[:, v % 2, :], ps[:, 6:8, :].rearrange("p a n -> p (a n)")).then_inc(S["xa_h"], 1)

            def xo_hi(v):
                j, u = divmod(v, 2)
                for b in range(2):
                    act.wait_ge(d_done[b], USE0["xa"] + v + 1)
                    copy(xqh[:, 2 * j + b, half(u)], ps[:, b, :]).then_inc(S["xo_h"], 1)
            xa_exp(0)
            v_turned(KB - 1)
            for m in range(2):
                act.dma_start(hs[:, m, :], s_h[m]).then_inc(S[f"hs_ld{m}"], 16)
            for v in range(2 * XH):
                xa_hi(v)
                if v + 1 < 2 * XH:
                    xa_exp(v + 1)
                if v:
                    xo_hi(v - 1)
            xo_hi(2 * XH - 1)

            for m in range(KB):
                for b in range(2):
                    square(1, m, b, USE0["xo"], hF, sq, f0h, "g_ffn")
                if m + 2 < KB:
                    act.dma_start(hs[:, m % 2, :], s_h[m + 2]).then_inc(S[f"hs_ld{m % 2}"], 16)
            acc_hi(1, acc, ach)
            act.wait_ge(d_done[1], USE0["xo"] + KB)
            for m in range(KB):
                copy(f1h[:, m, :], hF[:, m, H2:T], scale=smc("g_ffn", m)).then_inc(S["g1_h"], 1)
            rms(1)
            rms_copy(1, rbF)

            def channels(c, i, u):
                def tap(x_, b):
                    act.wait_ge(d_free[b], u + x_ + 1)
                    if not (isinstance(c, int) and c == 0):
                        act.wait_ge(S["c_lo"] if x_ else S["c_g"], 2 * c + b - 1)
                    y = yb if x_ else ya
                    apart(act, c)
                    act.activation(y[:, half(b)], z[:, 2 + b * H2:2 + (b + 1) * H2], ACT.Identity,
                                   scale=smc("cw2", c + FB * x_), bias=smc("b_conv", c + FB * x_)).then_inc(
                        S["c_y0"], 1)
                tap(0, 0)
                tap(0, 1)
                for b in range(2):
                    act.wait_ge(S["c_y"], 8 * c + 2 * b + 2)
                    act.activation(ya[:, half(b)], ya[:, half(b)], ACT.Silu).then_inc(S["c_s"], 1)
                tap(1, 0)
                tap(1, 1)
                for b in range(2):
                    act.wait_ge(S["c_g"], 2 * c + b + 1)
                    apart(act, i)
                    copy(blk(fah, i, b * H2, (b + 1) * H2), yb[:, half(b)]).then_inc(S["c_hi"], 1)
            c0, u = 0, FF_USE0
            for g, G in enumerate(FGROUPS):
                if g == 0:
                    channels(0, 0, FF_USE0)
                with act.Fori(int(g == 0), G) as i:
                    channels(c0 + i, i, u + 2 * i)
                c0, u = c0 + G, u + 2 * G + KB
            with act.Fori(0, KB) as m:
                for b in range(2):
                    square(2, m, b, FIN_USE0 - KB, hF, sq2)
                    copy(blk(yo, m, b * H2, (b + 1) * H2), blk(hF, m, b * H2, (b + 1) * H2),
                         scale=smc("g_final", m)).then_inc(S["o_y"], 1)
            acc_hi(2, acc2, ach2)
            rms(2)
            act.wait_ge(S["rb_r"], 3)
            for t in range(NT):
                act.wait_ge(d_done[0], FIN_USE0 + t + 1)
                if t >= 2:
                    act.wait_ge(S[f"out_st{t % 2}"], 16 * (t // 2))
                copy(orows[:, t % 2, 0:H2], ps[:, 0, :], scale=rsm[:, t, 0:1]).then_inc(d_free[0], 1)
                act.wait_ge(d_free[0], FIN_USE0 + t + 1)
                act.wait_ge(d_free[1], FIN_USE0 + t + 1)
                act.dma_start(out[t * P:(t + 1) * P, :], orows[:, t % 2, :]).then_inc(S[f"out_st{t % 2}"], 16)
            for b in range(2):
                act.wait_ge(S[f"out_st{b}"], 16 * (NT // 2))

        @block.vector
        def _(dve):
            def lo(o, full, h_):
                return dve.tensor_tensor(o, full, h_.bitcast(f32), ALU.subtract)

            def stt(o, a, s_, b_, op0, op1):
                return dve.scalar_tensor_tensor(out=o, in0=a, scalar=s_, in1=b_, op0=op0, op1=op1)

            dve.wait_ge(S["par"], 48)
            for o, n in ((ones_r, "ones"), (ident_r, "ident"), (mask_r, "mask")):
                dve.tensor_copy(o[:, :], cn[:, CN0[n]:CN0[n] + P]).then_inc(S["cst"], 1)
            dve.tensor_copy(posf[:, :], posi[:, :]).then_inc(S["cst"], 1)
            for b in range(2):
                c = slice(CH * b, CH * (b + 1))
                dve.wait_ge(S["x_std"], b + 1)
                dve.reciprocal(rst_x[:, c], rst_x[:, c]).then_inc(S["x_rs"], 1)
                dve.wait_ge(S["x_rs"], b + 1)
                for t in range(CH * b, CH * (b + 1)):
                    dve.tensor_scalar(xs[:, t, :], xs[:, t, :], rst_x[:, t:t + 1], None, ALU.mult).then_inc(
                        S["x_row"], 1)
            for n in range(2 * KB):
                b, k = n // KB, n % KB
                dve.wait_ge(S["xT_hi"], n + 1)
                stt(ul[:, k, half(b)], ps[:, 2 + n % 6, :], smc("g_mix", k), uh[:, k, half(b)].bitcast(f32), ALU.mult,
                    ALU.subtract).then_inc(S["xT_lo"], 1)
            step = [0]

            def link(ins):
                step[0] += 1
                ins.then_inc(S["angs"], 1)
                dve.wait_ge(S["angs"], step[0])

            inv = cn[:, CN0["inv"]:CN0["inv"] + NF]
            dve.wait_ge(S["cst"], 4)
            link(dve.tensor_tensor(ang[:, :, :], posf[:, :].unsqueeze(2).to_broadcast([P, NT, NF]),
                                   inv.unsqueeze(1).to_broadcast([P, NT, NF]), ALU.mult))
            link(dve.tensor_scalar(kk[:, :, :], ang[:, :, :], float(1 / (2 * np.pi)), 12582912.0, ALU.mult, ALU.add))
            link(dve.tensor_scalar(kk[:, :, :], kk[:, :, :], -12582912.0, None, ALU.add))
            for part in TWO_PI_PARTS:
                link(stt(ang[:, :, :].rearrange("p a n -> p (a n)"), kk[:, :, :].rearrange("p a n -> p (a n)"), -part,
                         ang[:, :, :].rearrange("p a n -> p (a n)"), ALU.mult, ALU.add))
            link(dve.tensor_scalar(ang[:, :, :], ang[:, :, :], PI, -PI, ALU.min, ALU.max))
            step_abs = stt(kk[:, :, :].rearrange("p a n -> p (a n)"), ang[:, :, :].rearrange("p a n -> p (a n)"), -1.0,
                           ang[:, :, :].rearrange("p a n -> p (a n)"), ALU.mult, ALU.max)
            step_abs.then_inc(S["sinr"], 1)
            dve.wait_ge(S["sinr"], 1)
            dve.tensor_scalar(kk[:, :, :], kk[:, :, :], -1.0, float(np.pi / 2), ALU.mult, ALU.add).then_inc(
                S["angs"], 1)

            def rotate(h, u):
                w = 2 * h + u
                dve.wait_ge(S["rows_qk"], w + 1)
                if isinstance(h, int) and w == 0:
                    dve.wait_ge(S["sins"], 2)
                at_least(dve, S["y_hi"], w - 1)
                at_least(dve, S["s_hi"], w)
                at_least(dve, S["kr_hi"], w)
                co, si = cosT[:, CH * u:CH * (u + 1), 0:R64], sinT[:, CH * u:CH * (u + 1), 0:R64]
                for n, (bank, dst, f, ta, tb) in enumerate(((2, rq, "xi", t1, t2), (3, rk, "zeta", t3, t4))):
                    src = ps[:, bank, :].rearrange("p (a two n) -> p a two n", a=CH, two=2)
                    o = dst[:, :].rearrange("p (a two n) -> p a two n", a=CH, two=2)
                    a_ = ta[:, :].rearrange("p (two a n) -> p two a n", a=CH, two=2)
                    b_ = tb[:, :].rearrange("p (two a n) -> p two a n", a=CH, two=2)
                    g = cnc(f, h)
                    stt(a_[:, 0], src[:, :, 0, :], g, co, ALU.mult, ALU.mult).then_inc(S["rot_t"], 1)
                    stt(b_[:, 0], src[:, :, 1, :], g, si, ALU.mult, ALU.mult).then_inc(S["rot_t"], 1)
                    stt(a_[:, 1], src[:, :, 1, :], g, co, ALU.mult, ALU.mult).then_inc(S["rot_t"], 1)
                    stt(b_[:, 1], src[:, :, 0, :], g, si, ALU.mult, ALU.mult).then_inc(S["rot_t"], 1)
                    dve.wait_ge(S["rot_t"], 8 * w + 4 * n + 4)
                    dve.tensor_tensor(o[:, :, 0, :], a_[:, 0], b_[:, 0], ALU.subtract)
                    l = dve.tensor_tensor(o[:, :, 1, :], a_[:, 1], b_[:, 1], ALU.add)
                l.then_inc(S["rot"], 1)

            def kr_lo(h, u):
                w = 2 * h + u
                dve.wait_ge(S["kr_hi"], w + 1)
                lo(krl[:, :], rk[:, :], krh[:, :]).then_inc(S["kr_lo"], 1)

            def qk_lo(h, u):
                dve.wait_ge(S["qk_hi"], 2 * h + u + 1)
                lo(qtl[:, :], ps[:, 2, :], qth[:, :])
                lo(ktl[:, :], ps[:, 3, :], kth[:, :]).then_inc(S["qk_lo"], 1)

            def v_lo(h, u):
                dve.wait_ge(S["v_hi"], 2 * h + u + 1)
                lo(vl[:, :], ps[:, 4, :], vh[:, :]).then_inc(S["v_lo"], 1)

            def mask_s(h, u):
                w = 2 * h + u
                dve.wait_ge(S["s_t"], w + 1)
                stt(t2[:, :].rearrange("p (a n) -> p a n", a=CH), ps[:, 5, :].rearrange("p (a n) -> p a n", a=CH),
                    cnc("ginv", h), tri.unsqueeze(1).to_broadcast([P, CH, P]), ALU.mult, ALU.mult).then_inc(S["s_m"], 1)

            def s_lo(h, u):
                dve.wait_ge(S["s_hi"], 2 * h + u + 1)
                lo(sl[:, :], t2[:, :], sh[:, :]).then_inc(S["s_lo"], 1)

            def states(h, u):
                w = 2 * h + u
                dve.wait_ge(S["kv_t"], w + 1)
                at_least(dve, S["r_hi"], w)
                if u == 0:
                    dve.memset(rst[:, 0, :], 0.0).then_inc(S["r_st"], 1)
                else:
                    dve.tensor_copy(rst[:, 0, :], rst[:, CH, :]).then_inc(S["r_st"], 1)
                for j in range(CH):
                    dve.wait_ge(S["r_st"], (CH + 1) * w + j + 1)
                    l = stt(rst[:, j + 1, :], rst[:, j, :], cnc("gC", h), ps[:, 4, j * P:(j + 1) * P], ALU.mult,
                            ALU.add).then_inc(S["r_st"], 1)

            def r_lo(h, u):
                dve.wait_ge(S["r_hi"], 2 * h + u + 1)
                lo(rsl[:, :], rst[:, 0:CH, :].rearrange("p a n -> p (a n)"), rsh[:, :]).then_inc(S["r_lo"], 1)

            def norm_y(h, u):
                w = 2 * h + u
                dve.wait_ge(S["y_t"], w + 1)
                at_least(dve, S["std"], w)
                for j in range(CH):
                    dve.bn_stats(bns[:, j, :], ps[:, 6, j * P:(j + 1) * P]).then_inc(S["gn_st"], 1)
                for j in range(CH):
                    dve.wait_ge(S["gn_st"], CH * w + j + 1)
                    apart(dve, h)
                    l = dve.bn_aggr(mvv[:, j, :], bns[:, j, :])
                l.then_inc(S["var"], 1)
                dve.wait_ge(S["std"], w + 1)
                dve.reciprocal(rsd[:, 1, :], rsd[:, 0, :]).then_inc(S["gn_rc"], 1)
                dve.wait_ge(S["gn_rc"], w + 1)
                for j in range(CH):
                    l = dve.tensor_scalar(yn[:, j * P:(j + 1) * P], ps[:, 6, j * P:(j + 1) * P], mvv[:, j, 0:1],
                                          rsd[:, 1, j:j + 1], ALU.subtract, ALU.mult)
                l.then_inc(S["yn_done"], 1)

            def gate_y(h, u):
                w = 2 * h + u
                dve.wait_ge(S["yT_t"], w + 1)
                dve.wait_ge(d_free[u], 4 * h + 4)
                at_least(dve, S["y_hi"], w)
                stt(t1[:, :], ps[:, 7, :], smc("g_ret", h), sg[:, half(u)], ALU.mult, ALU.mult).then_inc(
                    S["yg_done"], 1)
                dve.wait_ge(S["y_hi"], w + 1)
                lo(blk(ytl, h, u * H2, (u + 1) * H2), t1[:, :], blk(yth, h, u * H2, (u + 1) * H2)).then_inc(
                    S["y_lo"], 1)

            def order(h, last=False):
                old = (lambda f, u: None) if isinstance(h, int) and h == 0 else (lambda f, u: f(h - 1, u))
                new = (lambda f, u: None) if last else (lambda f, u: f(h, u))
                old(gate_y, 0)
                old(qk_lo, 1)
                old(v_lo, 1)
                old(mask_s, 1)
                old(s_lo, 1)
                old(states, 1)
                old(r_lo, 1)
                old(norm_y, 1)
                new(rotate, 0)
                new(kr_lo, 0)
                old(gate_y, 1)
                new(qk_lo, 0)
                new(v_lo, 0)
                new(mask_s, 0)
                new(s_lo, 0)
                new(states, 0)
                new(r_lo, 0)
                new(rotate, 1)
                new(kr_lo, 1)
                new(norm_y, 0)

            order(0)
            with dve.Fori(1, RH) as h:
                order(h)
            order(RH, last=True)

            def mul_r(i, first):
                for p in range(2):
                    m = 2 * i + p
                    for b in range(2):
                        dve.wait_ge(d_done[b], USE0["gr"] + 2 * m + 2)
                        dve.wait_ge(d_free[b], USE0["gr"] + 2 * m + 1)
                        if not first:
                            dve.wait_ge(S[f"m_st{p}"], 16 * i)
                        dve.tensor_tensor(mxr[:, p, half(b)], ps[:, b, :], sig[:, p, half(b)],
                                          ALU.mult).then_inc(d_free[b], 1)
            mul_r(0, True)
            with dve.Fori(1, KB // 2) as i:
                mul_r(i, False)

            dve.wait_ge(S["m_st0"], 16 * (KB // 2))
            dve.wait_ge(S["m_st1"], 16 * (KB // 2))
            dve.memset(krow[:, :, 0:NOPE], 0.0)
            for n in range(2 * QB):
                j, b = divmod(n, 2)
                dve.wait_ge(S["l_e"], n + 1)
                stt(cql[:, j, half(b)], ps[:, b, :], smc("g_q_lat", j), cqh[:, j, half(b)].bitcast(f32), ALU.mult,
                    ALU.subtract).then_inc(d_free[b], 1)
            dve.wait_ge(S["l_std"], 1)
            dve.reciprocal(lrq[:, :, :], lrq[:, :, :]).then_inc(S["l_rc"], 1)
            dve.wait_ge(S["l_std"], 2)
            dve.reciprocal(lr[:, :], lr[:, :]).then_inc(S["l_rc"], 1)
            dve.wait_ge(S["l_rc"], 2)
            for b in range(2):
                z_ = lz[:, QB, half(b)]
                stt(z_, z_, smc("g_kv_lat"), lr[:, half(b)], ALU.mult, ALU.mult).then_inc(S["l_c"], 1)
            dve.wait_ge(S["k_row"], 1)
            co, si = cosT[:, :, R64:NF], sinT[:, :, R64:NF]
            src = ps[:, 7, 0:NT * ROPE].rearrange("p (t two n) -> p t two n", t=NT, two=2)
            k1 = kr1[:, :, :].rearrange("p t (two n) -> p t two n", two=2)
            k2 = kr2[:, :, :].rearrange("p t (two n) -> p t two n", two=2)
            for c in range(2):
                dve.tensor_tensor(k1[:, :, c, :], src[:, :, c, :], co, ALU.mult).then_inc(S["k_r1"], 1)
                dve.tensor_tensor(k2[:, :, c, :], src[:, :, 1 - c, :], si, ALU.mult).then_inc(S["k_r1"], 1)
            dve.wait_ge(S["k_r1"], 4)
            dve.tensor_tensor(krow[:, :, NOPE:NOPE + R16], k1[:, :, 0, :], k2[:, :, 0, :], ALU.subtract).then_inc(
                S["k_r2"], 1)
            dve.tensor_tensor(krow[:, :, NOPE + R16:QK], k1[:, :, 1, :], k2[:, :, 1, :], ALU.add).then_inc(
                S["k_r2"], 2)
            for t in range(NT):
                for b in range(2):
                    dve.wait_ge(d_free[b], USE0["qrow"] + t + 1)
                at_least(dve, S["q_rope"], t)
                q = qrow[:, t, :].rearrange("p (h n) -> p h n", h=MH)
                x1, x2 = q[:, :, NOPE:NOPE + R16], q[:, :, NOPE + R16:QK]
                co = cosT[:, t, R64:NF].unsqueeze(1).to_broadcast([P, MH, R16])
                si = sinT[:, t, R64:NF].unsqueeze(1).to_broadcast([P, MH, R16])
                dve.tensor_tensor(qr1[:, :, 0:R16], x1, co, ALU.mult).then_inc(S["q_r1"], 1)
                dve.tensor_tensor(qr1[:, :, R16:ROPE], x2, co, ALU.mult).then_inc(S["q_r1"], 1)
                dve.tensor_tensor(qr2[:, :, 0:R16], x2, si, ALU.mult).then_inc(S["q_r1"], 1)
                dve.tensor_tensor(qr2[:, :, R16:ROPE], x1, si, ALU.mult).then_inc(S["q_r1"], 1)
                dve.wait_ge(S["q_r1"], 4 * t + 4)
                dve.tensor_tensor(x1, qr1[:, :, 0:R16], qr2[:, :, 0:R16], ALU.subtract)
                dve.tensor_tensor(x2, qr1[:, :, R16:ROPE], qr2[:, :, R16:ROPE], ALU.add).then_inc(S["q_rope"], 1)
                if t == 2:
                    for b in range(2):
                        dve.wait_ge(S["l_hi"], b + 1)
                        lo(ckl[:, half(b)], lz[:, QB, half(b)], ckh[:, half(b)]).then_inc(S["l_lo"], 1)
            R = slice(NOPE, QK)
            for b in range(2):
                dve.wait_ge(S["k_hi"], 2 * b + 2)
                for p in range(2):
                    lo(kbl[R, p, half(b)], ps[R, 6 + b, :], kbh[R, p, half(b)]).then_inc(S["k_lo"], 1)
            for t in range(NT):
                dve.wait_ge(S["v_evh"], t + 1)
                lo(vrl[:, t, :], ps[:, t % 2, :], vrh[:, t, :]).then_inc(d_free[t % 2], 1)

            def aux_lo(h, n):
                dve.wait_ge(S["aux_hi"], USE_OF["aux", h, n] + 1)
                b = n % 2
                r = slice(0, NOPE) if n < 2 else slice(0, QK)
                if n < 2:
                    lo(kbl[r, h % 2, half(b)], ps[r, 0, :], kbh[r, h % 2, half(b)]).then_inc(S["aux_lo"], 1)
                else:
                    lo(mql[r, b, :], ps[r, 0, :], mqh[r, b, :]).then_inc(S["aux_lo"], 1)

            def o_lo(fb, b):
                dve.wait_ge(S["o_hi"], 2 * fb + b + 1)
                lo(otl[:, fb, half(b)], oT[:, fb, half(b)], oth[:, fb, half(b)]).then_inc(S["o_lo"], 1)

            def m_max(w):
                n = (UNITS[w][1] + 1) * P
                c = 2 + 2 * (w % 2)
                dve.wait_ge(S["m_s"], w + 1)
                at_least(dve, S["m_exp"], w - 1)
                dve.tensor_reduce(amax[:, 0, w % 4:w % 4 + 1], ps[:, c:c + 2, :].rearrange("p a n -> p (a n)")[:, 0:n], AX.X,
                                  ALU.max).then_inc(S["m_mx"], 1)
                dve.wait_ge(S["m_mx"], w + 1)
                dve.tensor_scalar(aneg[:, 0, w % 4:w % 4 + 1], amax[:, 0, w % 4:w % 4 + 1], -QK ** -0.5, None, ALU.mult).then_inc(
                    S["m_neg"], 1)

            def m_ptl(w):
                i, g = UNITS[w][1], w // CH
                for n in range(i // CH + 1):
                    q = PIECE0[w] + n
                    c0, c1 = CH * n, min(CH * (n + 1), i + 1)
                    at = (slice(None), slice(c0, c1), slice(i % CH * P, (i % CH + 1) * P))
                    dve.wait_ge(S["m_pth"], q + 1)
                    lo((p1l if g % 2 else p0l)[at],
                       ps[:, 6 + q % 2, 0:(c1 - c0) * P].rearrange("p (a n) -> p a n", n=P),
                       (p1h if g % 2 else p0h)[at]).then_inc(S["m_ptl"], 1)

            def m_inv(w):
                dve.wait_ge(S["m_exp"], w + 1)
                dve.reciprocal(ainv[:, w // CH % 2, w % CH:w % CH + 1], asum[:, 0, w % CH:w % CH + 1]).then_inc(
                    S["m_ri"], 1)

            def m_out(g):
                h, b = divmod(g, 2)
                r = slice(h % 2 * DV, (h % 2 + 1) * DV)
                o = oT[r, h // 2, half(b)]
                dve.wait_ge(S["m_pv"], g + 1)
                dve.wait_ge(S["aux_hi"], USE_OF["sum", g] + 1)
                dve.tensor_tensor(o, ps[r, 1, :], o, ALU.mult).then_inc(S["aux_lo"], 1)
            for n in range(4):
                aux_lo(0, n)
            NW = len(UNITS)
            m_max(0)
            m_max(1)
            m_inv(0)
            for w in range(NW):
                h, r = divmod(w, NT)
                if w > CH and w % CH == 1:
                    m_out(w // CH - 1)
                m_ptl(w)
                if r in AUX_AT and h + 1 < MH:
                    aux_lo(h + 1, AUX_AT[r])
                if w + 2 < NW:
                    m_max(w + 2)
                if w + 1 < NW:
                    m_inv(w + 1)
                if h == MH - 1 and r < 4:
                    o_lo(r // 2, r % 2)
                if h == MH - 1 and r >= 6:
                    o_lo(2, r - 6)
            m_out(2 * MH - 1)
            for b in range(2):
                o_lo(3, b)

            for m in range(KB):
                dve.wait_ge(S[f"sa_ld{m % 2}"], 16 * (m // 2 + 1))
                dve.wait_ge(S[f"mr_ld{m % 2}"], 16 * (m // 2 + 1))
                for b in range(2):
                    a_ = sab[:, m % 2, half(b)]
                    dve.wait_ge(d_done[b], USE0["mix"] + m + 1)
                    dve.tensor_tensor(a_, ps[:, b, :], a_, ALU.mult).then_inc(d_free[b], 1)
                    dve.wait_ge(d_free[b], USE0["mix"] + m + 1)
                    dve.tensor_tensor(a_, a_, mrb[:, m % 2, half(b)], ALU.add).then_inc(S["mix_m"], 1)
                    dve.wait_ge(S["mix_hi"], 2 * m + b + 1)
                    lo(mil[:, m, half(b)], a_, mih[:, m, half(b)]).then_inc(S["mix_lo"], 1)

            def resid(n, m, u, h_, res, acc_, sq_, gh=None, gl=None, gname=None):
                for b in range(2):
                    dve.wait_ge(d_done[b], u)
                    hb = blk(h_, m, b * H2, (b + 1) * H2)
                    dve.tensor_tensor(hb, ps[:, b, :], res(b), ALU.add).then_inc(d_free[b], 1)
                    q = 2 * KB * n + 2 * m + b
                    if gh is not None and b == 0:
                        dve.wait_ge(S["o_gh"], KB * n + m + 1)
                        stt(blk(gl, m, 0, H2), hb, smc(gname, m), blk(gh, m, 0, H2).bitcast(f32), ALU.mult,
                            ALU.subtract).then_inc(S["o_gl"], 1)
                    dve.wait_ge(S["o_sq"], q + 1)
                    at_least(dve, S["o_ac"], q - 1)
                    dve.tensor_tensor(acc_[:, b, :], acc_[:, b, :], sq_[:, b, :], ALU.add).then_inc(S["o_ac"], 1)

            def acc_lo(n, acc_, ach_, acl_):
                dve.wait_ge(S["ac_h"], n + 1)
                lo(acl_[:, :, :], acc_[:, :, :], ach_[:, :, :]).then_inc(S["ac_l"], 1)

            def rms_inv(n):
                dve.wait_ge(S["ss_s"], n + 1)
                dve.reciprocal(rsm[:, :, :], rsm[:, :, :]).then_inc(S["rb_r"], 1)

            def clear(n, acc_):
                dve.memset(acc_[:, :, :], 0.0).then_inc(S["o_z"], 1)
                dve.wait_ge(S["o_z"], n + 1)

            def g1_lo(n, h_, gh, gl, gname):
                for m in range(KB):
                    dve.wait_ge(S["g1_h"], KB * n + m + 1)
                    stt(gl[:, m, :], h_[:, m, H2:T], smc(gname, m), gh[:, m, :].bitcast(f32), ALU.mult,
                        ALU.subtract).then_inc(S["g1_l"], 1)

            def h0_block(m):
                resid(0, m, USE0["out"] + m + 1, hT, lambda b: blk(hT, m, b * H2, (b + 1) * H2), acc, sq, g0h, g0l,
                      "g_cross")
            clear(0, acc)
            h0_block(0)
            with dve.Fori(1, KB) as m:
                h0_block(m)
            acc_lo(0, acc, ach, acl)
            g1_lo(0, hT, g1h, g1l, "g_cross")
            rms_inv(0)

            dve.wait_ge(S["rb_c"], 1)

            def xq_block(m):
                for b in range(2):
                    dve.wait_ge(d_done[b], USE0["xq"] + m + 1)
                    dve.tensor_tensor(xf[:, b, :], ps[:, b, :], rbc[:, b, :], ALU.mult).then_inc(
                        d_free[b], 1)
                    dve.wait_ge(S["xq_h"], 2 * m + b + 1)
                    lo(blk(xql, m, b * H2, (b + 1) * H2), xf[:, b, :], blk(xqh, m, b * H2, (b + 1) * H2)).then_inc(
                        S["xq_l"], 1)
            with dve.Fori(0, KB - SLOTS) as m:
                xq_block(m)
            dve.wait_ge(S["mm_st"], 1)
            dve.reciprocal(mst[:, 2, :], mst[:, 1, :]).then_inc(S["mm_rc"], 1)
            dve.wait_ge(S["mm_rc"], 1)
            for r in range(MB):
                dve.tensor_scalar(mrow[:, r, :], mrow[:, r, :], mst[:, 2, r:r + 1], None, ALU.mult).then_inc(
                    S["mm_n"], 1)
            with dve.Fori(KB - SLOTS, KB) as m:
                xq_block(m)
            for k in range(KB):
                dve.wait_ge(S["mm_hi"], 2 * (k // 2) + 2)
                c = (k % 2) * NMEM
                stt(mtl[:, k, :], ps[:, 4 + k // 2, c:c + NMEM], smc("g_mem", k), mth[:, k, :].bitcast(f32), ALU.mult,
                    ALU.subtract).then_inc(S["mm_lo"], 1)
            with dve.Fori(0, KB // 2) as i:
                for b in range(2):
                    dve.wait_ge(S["kv_h"], 2 * i + b + 1)
                    lo(blk(mkl, 2 * i + b, 0, NMEM), ps[:, b, 0:NMEM], blk(mkh, 2 * i + b, 0, NMEM)).then_inc(
                        d_free[b], 1)

            def v_turned(m):
                dve.wait_ge(S["mv_h"], m + 1)
                lo(mvl[:, :, m * P:(m + 1) * P], ps[:, 4, 0:NMEM].rearrange("p (r n) -> p r n", r=MB),
                   mvh[:, :, m * P:(m + 1) * P]).then_inc(S["mv_l"], 1)
            for m in range(KB - 1):
                v_turned(m)

            def xa_max(v):
                c = 2 if v % 2 == 0 else 4
                dve.wait_ge(S["xa_s"], v + 1)
                at_least(dve, S["xa_e"], v - 1)
                if v == 0:
                    dve.wait_ge(S["m_exp"], NW)
                dve.tensor_reduce(amax[:, v % 2, :], ps[:, c:c + 2, :].rearrange("p a (t n) -> p (a t) n", t=2), AX.X,
                                  ALU.max).then_inc(S["xa_m"], 1)
                dve.wait_ge(S["xa_m"], v + 1)
                dve.tensor_scalar(aneg[:, v % 2, :], amax[:, v % 2, :], -XD ** -0.5, None, ALU.mult).then_inc(
                    S["xa_n"], 1)

            def xa_norm(v):
                dve.wait_ge(S["xa_e"], v + 1)
                dve.reciprocal(ainv[:, v % 2, :], asum[:, v % 2, :]).then_inc(S["xa_r"], 1)
                dve.wait_ge(S["xa_r"], v + 1)
                for t in range(CH):
                    l = dve.tensor_scalar(pr[:, v % 2, t, :], pr[:, v % 2, t, :], ainv[:, v % 2, t:t + 1], None,
                                          ALU.mult)
                l.then_inc(S["xa_p"], 1)

            def xa_lo(v):
                dve.wait_ge(S["xa_h"], v + 1)
                lo(xpl[:, v % 2, :], ps[:, 6:8, :].rearrange("p a n -> p (a n)"), xph[:, v % 2, :]).then_inc(
                    S["xa_l"], 1)

            def xo_lo(v):
                j, u = divmod(v, 2)
                for b in range(2):
                    dve.wait_ge(S["xo_h"], 2 * v + b + 1)
                    lo(xql[:, 2 * j + b, half(u)], ps[:, b, :], xqh[:, 2 * j + b, half(u)]).then_inc(
                        d_free[b], 1)
            xa_max(0)
            v_turned(KB - 1)
            xa_norm(0)
            for v in range(2 * XH):
                if v + 1 < 2 * XH:
                    xa_max(v + 1)
                xa_lo(v)
                if v:
                    xo_lo(v - 1)
                if v + 1 < 2 * XH:
                    xa_norm(v + 1)
            xo_lo(2 * XH - 1)

            clear(1, acc)
            for m in range(KB):
                dve.wait_ge(S[f"hs_ld{m % 2}"], 16 * (m // 2 + 1))
                resid(1, m, USE0["xo"] + m + 1, hF, lambda b: hs[:, m % 2, half(b)], acc, sq, f0h, f0l, "g_ffn")
            acc_lo(1, acc, ach, acl)
            g1_lo(1, hF, f1h, f1l, "g_ffn")
            rms_inv(1)
            dve.memset(z[:, 0:2], 0.0).then_inc(S["c_zp"], 1)
            dve.wait_ge(S["c_zp"], 1)
            dve.wait_ge(S["rb_c"], 2)

            def channels(c, i, u):
                def conv(x_, b):
                    q = 4 * c + 2 * x_ + b
                    y = (yb if x_ else ya)[:, half(b)]
                    dve.wait_ge(d_done[b], u + x_ + 1)
                    if x_ or b or not isinstance(c, int):
                        dve.wait_ge(S["c_y"], 2 * q)
                    dve.tensor_tensor(z[:, 2 + b * H2:2 + (b + 1) * H2], ps[:, b, :], rbF[:, b, :],
                                      ALU.mult).then_inc(d_free[b], 1)
                    dve.wait_ge(S["c_y0"], q + 1)
                    stt(y, z[:, 1 + b * H2:1 + (b + 1) * H2], smc("cw1", c + FB * x_), y, ALU.mult, ALU.add).then_inc(
                        S["c_y"], 1)
                    dve.wait_ge(S["c_y"], 2 * q + 1)
                    stt(y, z[:, b * H2:(b + 1) * H2], smc("cw0", c + FB * x_), y, ALU.mult, ALU.add).then_inc(
                        S["c_y"], 1)
                conv(0, 0)
                conv(0, 1)
                conv(1, 0)
                conv(1, 1)
                for b in range(2):
                    y = yb[:, half(b)]
                    dve.wait_ge(S["c_s"], 2 * c + b + 1)
                    dve.wait_ge(S["c_y"], 8 * c + 4 + 2 * b + 2)
                    dve.tensor_tensor(y, y, ya[:, half(b)], ALU.mult).then_inc(S["c_g"], 1)
                for b in range(2):
                    y = yb[:, half(b)]
                    dve.wait_ge(S["c_hi"], 2 * c + b + 1)
                    lo(blk(fal, i, b * H2, (b + 1) * H2), y, blk(fah, i, b * H2, (b + 1) * H2)).then_inc(S["c_lo"], 1)

            c0, u = 0, FF_USE0
            for g, G in enumerate(FGROUPS):
                if g == 0:
                    channels(0, 0, u)
                with dve.Fori(int(g == 0), G) as i:
                    channels(c0 + i, i, u + 2 * i)
                c0, u = c0 + G, u + 2 * G
                if g < len(FGROUPS) - 1:
                    with dve.Fori(0, KB) as m:
                        for b in range(2):
                            hb = blk(hF, m, b * H2, (b + 1) * H2)
                            dve.wait_ge(d_done[b], u + m + 1)
                            dve.tensor_tensor(hb, ps[:, b, :], hb, ALU.add).then_inc(d_free[b], 1)
                else:
                    dve.wait_ge(d_done[0], u + 1)
                    clear(2, acc2)
                    with dve.Fori(0, KB) as m:
                        resid(2, m, u + m + 1, hF, lambda b: blk(hF, m, b * H2, (b + 1) * H2), acc2, sq2)
                u += KB
            acc_lo(2, acc2, ach2, acl2)
            rms_inv(2)
            dve.wait_ge(S["rb_r"], 3)
            for t in range(NT):
                dve.wait_ge(d_done[1], FIN_USE0 + t + 1)
                if t >= 2:
                    dve.wait_ge(S[f"out_st{t % 2}"], 16 * (t // 2))
                dve.tensor_scalar(orows[:, t % 2, H2:D], ps[:, 1, :], rsm[:, t, 0:1], None, ALU.mult).then_inc(
                    d_free[1], 1)


def weight_slabs(w_in, w_uq, w_ukv, w_proj_mla, w_proj_ret, w_out, w_xq, w_xkv, w_xo, w_up, w_down):
    out = np.zeros((NSLAB, P, 1024), np.float32)
    n = 0

    def put(w):
        nonlocal n
        k, m = w.shape
        out[n, :, :k // P * m] = w.reshape(k // P, P, m).transpose(1, 0, 2).reshape(P, -1)
        n += 1

    def cols(w, m, width=P):
        return w[:, m * width:(m + 1) * width]
    for h in range(RH):
        for c in (C_RQ, C_RK, C_RV, C_RG):
            put(w_in[:, c + h * RDK:c + (h + 1) * RDK])
    for m in range(KB):
        put(w_in[:, C_GA + m * P:C_GA + (m + 1) * P])
    for m in range(KB):
        put(w_in[:, C_GR + m * P:C_GR + (m + 1) * P])
        put(cols(w_proj_ret, m))
    for c, e in ((0, P), (P, QR), (C_KV, C_KR), (C_KR, C_RQ)):
        put(w_in[:, c:e])
    put(w_uq[0:P])
    put(w_uq[P:QR])
    kv = w_ukv.reshape(KVR, MH, NOPE + DV)
    put(kv[:, :, :NOPE].reshape(KVR, -1))
    put(kv[:, :, NOPE:].reshape(KVR, -1))
    for m in range(KB // 2):
        put(cols(w_proj_mla, m, 2 * P))
    for w, c in ((w_out, KB), (w_xq, KB), (w_xkv, 2 * KB), (w_xo, KB)):
        for m in range(c):
            put(cols(w, m))
    c0 = 0
    for g in FGROUPS:
        for c in range(c0, c0 + g):
            put(cols(w_up, c))
            put(cols(w_up, FB + c))
        for m in range(KB):
            put(cols(w_down[c0 * P:(c0 + g) * P], m))
        c0 += g
    assert n == NSLAB
    return out


def constants():
    g = 1.0 - np.exp2(-5.0 - np.arange(RH))
    i = np.arange(P)[:, None]
    parts = {
        "ident": np.eye(P), "tri": np.triu(np.ones((P, P))),
        "mask": np.where(np.arange(P)[None, :] > i, -1e30, 0.0), "ones": np.ones((P, P)),
        "inv": np.broadcast_to(np.concatenate([10000.0 ** -(np.arange(n) / n) for n in (R64, R16)]), (P, NF)),
        "xi": g ** (i + 1.0), "zeta": g ** (P - 1.0 - i) * RDK ** -0.5,
        "ginv": np.broadcast_to(g ** -float(P), (P, RH)), "gC": np.broadcast_to(g ** float(P), (P, RH)),
        "eps": np.full((P, 1), EPS)}
    return np.concatenate([parts[k] for k in CN0], axis=1).astype(np.float32)


def kernel(x, mem, positions, g_mix, w_in, b_gate, g_q_lat, w_uq, g_kv_lat, w_ukv, w_proj_mla, g_ret, w_proj_ret,
           w_out, g_cross, g_mem, w_xq, w_xkv, w_xo, g_ffn, w_up, w_conv, b_conv, w_down, g_final):
    import concourse.bacc as bacc
    from concourse.bass_utils import run_bass_kernel_spmd

    a = np.asarray
    w_conv = a(w_conv)[0]
    small = {"g_mix": a(g_mix)[0], "g_cross": a(g_cross)[0], "g_ffn": a(g_ffn)[0], "g_final": a(g_final),
             "g_mem": a(g_mem)[0], "b_gate": a(b_gate)[0], "g_q_lat": a(g_q_lat)[0], "g_kv_lat": a(g_kv_lat)[0],
             "g_ret": a(g_ret)[0], "cw0": w_conv[0], "cw1": w_conv[1], "cw2": w_conv[2], "b_conv": a(b_conv)[0]}
    arrays = {
        "x": np.ascontiguousarray(a(x)[0]), "mem": np.ascontiguousarray(a(mem)[0]),
        "pos": np.ascontiguousarray(a(positions)[0].reshape(NT, P).T),
        "slabs": weight_slabs(*(a(w)[0] for w in (w_in, w_uq, w_ukv, w_proj_mla, w_proj_ret, w_out, w_xq, w_xkv, w_xo,
                                                  w_up, w_down))),
        "small": np.ascontiguousarray(np.concatenate([small[k].reshape(-1, P).T for k, _ in SMALL], axis=1)),
        "const": constants()}
    nc = bacc.Bacc("TRN2", target_bir_lowering=False, num_devices=1)
    args = [nc.dram_tensor(f"in_{k}", v.shape, mybir.dt.from_np(v.dtype), kind="ExternalInput").ap()
            for k, v in arrays.items()]
    out = nc.dram_tensor("out", (T, D), mybir.dt.float32, kind="ExternalOutput").ap()
    build(nc, *args, out)
    r = run_bass_kernel_spmd(nc, [{f"in_{k}": v for k, v in arrays.items()}], core_ids=[0])
    return r.results[0]["out"].reshape(1, T, D)
```
